# Optimizing a Trainium2 kernel written in Bass

```python
import math
import jax, jax.numpy as jnp
from jax import lax
import numpy as np

D_MODEL = 1024
BATCH = 1
SEQ = 512
DEPTH = 1

HEAD_DIM = 64
D_ATTN = D_MODEL // 2
D_RWKV = D_MODEL - D_ATTN
D_MIX = D_ATTN + D_RWKV
N_ATTN_HEADS = D_ATTN // HEAD_DIM
N_RWKV_HEADS = D_RWKV // HEAD_DIM
DILATED_BRANCHES = ((128, 1), (512, 4), (2048, 16))
Q_BLOCK = 128
LORA_DECAY = 32
LORA_AAA = 32
LORA_MV = 32
LORA_GATE = 96
D_FF = 4 * D_MODEL
NORM_EPS = 1e-6
GN_EPS = 64e-5
N_SHIFT = 3 * D_RWKV + LORA_DECAY + LORA_AAA + LORA_GATE
N_COLS_FIRST = 3 * D_ATTN + N_SHIFT
N_COLS_REST = N_COLS_FIRST + LORA_MV


def _rms_norm(x, g):
    xf = x.astype(jnp.float32)
    y = xf * lax.rsqrt(jnp.mean(xf * xf, axis=-1, keepdims=True) + NORM_EPS)
    return (y * g.astype(jnp.float32)).astype(x.dtype)

def _token_shift(z, mu):
    prev = jnp.pad(z, ((0, 0), (1, 0), (0, 0)))[:, :-1]
    return z + (prev - z) * mu

def _dilated_branch(q, k, v, window, dilation):
    B, S, H, Dh = q.shape
    L = S // dilation
    K = window // dilation
    qb = math.gcd(L, Q_BLOCK)
    nb = L // qb

    def phase(t):
        return t.reshape(B, L, dilation, H, Dh).transpose(0, 2, 3, 1, 4)

    qs, ks, vs = phase(q), phase(k), phase(v)
    pad = ((0, 0), (0, 0), (0, 0), (K, 0), (0, 0))
    kp, vp = jnp.pad(ks, pad), jnp.pad(vs, pad)
    idx = jnp.arange(nb)[:, None] * qb + jnp.arange(qb + K)[None, :]
    kb = kp[:, :, :, idx, :]
    vb = vp[:, :, :, idx, :]
    qblk = qs.reshape(B, dilation, H, nb, qb, Dh)
    s = jnp.einsum('bdhnqc,bdhnkc->bdhnqk', qblk, kb) * (1.0 / math.sqrt(Dh))
    j = jnp.arange(qb)[:, None]
    m_idx = jnp.arange(qb + K)[None, :]
    dist = j + K - m_idx
    blk = jnp.arange(nb)[:, None, None]
    valid = (dist >= 0) & (dist <= K) & (blk * qb + m_idx - K >= 0)
    s = jnp.where(valid, s, -jnp.inf)
    m = jnp.max(s, axis=-1)
    p = jnp.exp(s - m[..., None])
    l = jnp.sum(p, axis=-1)
    acc = jnp.einsum('bdhnqk,bdhnkc->bdhnqc', p, vb)
    acc = acc.reshape(B, dilation, H, L, Dh).transpose(0, 3, 1, 2, 4).reshape(B, S, H, Dh)
    m = m.reshape(B, dilation, H, L).transpose(0, 3, 1, 2).reshape(B, S, H)
    l = l.reshape(B, dilation, H, L).transpose(0, 3, 1, 2).reshape(B, S, H)
    return m, l, acc

def _dilated_attention(q, k, v):
    B, S, _ = q.shape
    heads = lambda t: t.astype(jnp.float32).reshape(B, S, N_ATTN_HEADS, HEAD_DIM)
    qh, kh, vh = heads(q), heads(k), heads(v)
    outs = [_dilated_branch(qh, kh, vh, w, d) for (w, d) in DILATED_BRANCHES]
    m_all = jnp.maximum(jnp.maximum(outs[0][0], outs[1][0]), outs[2][0])
    num = sum(jnp.exp(m - m_all)[..., None] * acc for (m, l, acc) in outs)
    den = sum(jnp.exp(m - m_all) * l for (m, l, acc) in outs)
    o = num / den[..., None]
    return o.reshape(B, S, D_ATTN).astype(q.dtype)

def _rwkv7_scan(r, w, k, v, kk, b):
    B, S, H, N = r.shape

    def step(state, inp):
        r_t, w_t, k_t, v_t, kk_t, b_t = inp
        sa = jnp.einsum('bhij,bhj->bhi', state, kk_t)
        state = (state * w_t[:, :, None, :]
                 - sa[..., None] * b_t[:, :, None, :]
                 + v_t[..., None] * k_t[:, :, None, :])
        y = jnp.einsum('bhij,bhj->bhi', state, r_t)
        return state, y

    xs = tuple(jnp.moveaxis(t, 1, 0) for t in (r, w, k, v, kk, b))
    state0 = jnp.zeros((B, H, N, N), jnp.float32)
    _, ys = lax.scan(step, state0, xs)
    return jnp.moveaxis(ys, 0, 1)

def _rwkv7(r, k, v, xw, xa, xg, w0, w_up, a0, a_up, g_up, k_k, k_a, r_k, gn_w, gn_b):
    B, S, _ = r.shape
    H, N = N_RWKV_HEADS, HEAD_DIM
    f32 = jnp.float32
    heads = lambda t: t.astype(f32).reshape(B, S, H, N)
    logw = -jax.nn.softplus(-(w0 + jnp.tanh(xw) @ w_up).astype(f32)) - 0.5
    decay = jnp.exp(-jnp.exp(logw))
    a = jax.nn.sigmoid((a0 + xa @ a_up).astype(f32))
    g = (jax.nn.sigmoid(xg) @ g_up).astype(f32)
    kk = heads(k * k_k)
    kk = kk / jnp.maximum(jnp.sqrt(jnp.sum(kk * kk, axis=-1, keepdims=True)), 1e-12)
    k_mod = k.astype(f32) * (1.0 + (a - 1.0) * k_a.astype(f32))
    rh, kh, vh, ah, wh = heads(r), heads(k_mod), heads(v), heads(a), heads(decay)
    y = _rwkv7_scan(rh, wh, kh, vh, kk, kk * ah)
    mean = jnp.mean(y, axis=-1, keepdims=True)
    var = jnp.mean(jnp.square(y - mean), axis=-1, keepdims=True)
    yn = ((y - mean) * lax.rsqrt(var + GN_EPS)).reshape(B, S, D_RWKV)
    yn = yn * gn_w.astype(f32) + gn_b.astype(f32)
    bonus = jnp.sum(rh * kh * r_k.astype(f32), axis=-1, keepdims=True) * vh
    out = (yn + bonus.reshape(B, S, D_RWKV)) * g
    return out.astype(r.dtype)

def first_inputs(seed: int = 0) -> dict:
    key = jax.random.key(seed)
    ks = iter(jax.random.split(key, 40))
    f32 = jnp.float32
    nrm = lambda shape, scale: jax.random.normal(next(ks), shape, f32) * scale
    gain = lambda shape: 1.0 + nrm(shape, 0.05)
    L1 = DEPTH - 1
    return {
        "x": nrm((BATCH, SEQ, D_MODEL), 1.0),
        "norm_mix_pre": gain((DEPTH, D_MODEL)),
        "norm_mix_post": gain((DEPTH, D_MODEL)),
        "norm_ffn_pre": gain((DEPTH, D_MODEL)),
        "norm_ffn_post": gain((DEPTH, D_MODEL)),
        "w_in_first": nrm((D_MODEL, N_COLS_FIRST), D_MODEL ** -0.5),
        "w_in_rest": nrm((L1, D_MODEL, N_COLS_REST), D_MODEL ** -0.5),
        "mu_shift": jax.random.uniform(next(ks), (DEPTH, N_SHIFT), f32),
        "mu_shift_mv": jax.random.uniform(next(ks), (L1, LORA_MV), f32),
        "attn_out_gain": gain((DEPTH, D_ATTN)),
        "decay_w0": jax.random.uniform(next(ks), (DEPTH, D_RWKV), f32, -5.0, 0.0),
        "decay_up": nrm((DEPTH, LORA_DECAY, D_RWKV), 0.5 * LORA_DECAY ** -0.5),
        "aaa_a0": nrm((DEPTH, D_RWKV), 0.1),
        "aaa_up": nrm((DEPTH, LORA_AAA, D_RWKV), 0.5 * LORA_AAA ** -0.5),
        "mv_v0": nrm((L1, D_RWKV), 0.5),
        "mv_up": nrm((L1, LORA_MV, D_RWKV), 0.5 * LORA_MV ** -0.5),
        "gate_up": nrm((DEPTH, LORA_GATE, D_RWKV), LORA_GATE ** -0.5),
        "k_k": 0.85 + nrm((DEPTH, D_RWKV), 0.1),
        "k_a": 1.0 + nrm((DEPTH, D_RWKV), 0.1),
        "r_k": nrm((DEPTH, N_RWKV_HEADS, HEAD_DIM), 0.1),
        "gn_w": gain((DEPTH, D_RWKV)),
        "gn_b": nrm((DEPTH, D_RWKV), 0.02),
        "w_out": nrm((DEPTH, D_MIX, D_MODEL), D_MIX ** -0.5),
        "w_ffn_up": nrm((DEPTH, D_MODEL, D_FF), D_MODEL ** -0.5),
        "w_ffn_down": nrm((DEPTH, D_FF, D_MODEL), D_FF ** -0.5),
    }

def first_block(x, norm_mix_pre, norm_mix_post, norm_ffn_pre, norm_ffn_post,
              w_in_first, w_in_rest, mu_shift, mu_shift_mv, attn_out_gain,
              decay_w0, decay_up, aaa_a0, aaa_up, mv_v0, mv_up, gate_up,
              k_k, k_a, r_k, gn_w, gn_b, w_out, w_ffn_up, w_ffn_down):
    v_first = None
    o0, o1, o2 = 3 * D_RWKV, 3 * D_RWKV + LORA_DECAY, 3 * D_RWKV + LORA_DECAY + LORA_AAA
    for i in range(DEPTH):
        h = _rms_norm(x, norm_mix_pre[i])
        z = h @ (w_in_first if i == 0 else w_in_rest[i - 1])
        q = z[..., 0:D_ATTN]
        k = z[..., D_ATTN:2 * D_ATTN]
        v = z[..., 2 * D_ATTN:3 * D_ATTN]
        zs = _token_shift(z[..., 3 * D_ATTN:3 * D_ATTN + N_SHIFT], mu_shift[i])
        r_r = zs[..., 0:D_RWKV]
        k_r = zs[..., D_RWKV:2 * D_RWKV]
        v_r = zs[..., 2 * D_RWKV:3 * D_RWKV]
        xw = zs[..., o0:o1]
        xa = zs[..., o1:o2]
        xg = zs[..., o2:N_SHIFT]
        if i == 0:
            v_first = v_r
        else:
            xmv = _token_shift(z[..., N_COLS_FIRST:], mu_shift_mv[i - 1])
            vgate = jax.nn.sigmoid(mv_v0[i - 1] + xmv @ mv_up[i - 1])
            v_r = v_r + (v_first - v_r) * vgate
        attn = _rms_norm(_dilated_attention(q, k, v), attn_out_gain[i])
        rw = _rwkv7(r_r, k_r, v_r, xw, xa, xg, decay_w0[i], decay_up[i], aaa_a0[i],
                    aaa_up[i], gate_up[i], k_k[i], k_a[i], r_k[i], gn_w[i], gn_b[i])
        mixed = jnp.concatenate([attn, rw], axis=-1) @ w_out[i]
        x = x + _rms_norm(mixed, norm_mix_post[i])
        h = _rms_norm(x, norm_ffn_pre[i])
        f = jnp.square(jax.nn.relu(h @ w_ffn_up[i])) @ w_ffn_down[i]
        x = x + _rms_norm(f, norm_ffn_post[i])
    return x


N_ATTN_HEADS_2 = 8
ATTN_WIDTH = N_ATTN_HEADS_2 * HEAD_DIM
POOL_WIDTH = D_MODEL - ATTN_WIDTH
POOL_WINDOWS = (2, 4, 8, 16)
N_POOL_GROUPS = len(POOL_WINDOWS)
POOL_GROUP = POOL_WIDTH // N_POOL_GROUPS
IN_WIDTH = 3 * ATTN_WIDTH + POOL_WIDTH
MOBA_BLOCK = 256
MOBA_TOPK = 3
QUERY_CHUNK = 32
D_FF_2 = 4 * D_MODEL
EPS = 1e-6


def _alibi_slopes(n_heads):
    return jnp.asarray(2.0 ** (-8.0 * np.arange(1, n_heads + 1) / n_heads), dtype=jnp.float32)

def rms_norm(x, g):
    xf = x.astype(jnp.float32)
    y = xf * lax.rsqrt(jnp.mean(xf * xf, axis=-1, keepdims=True) + EPS)
    return (y * g.astype(jnp.float32)).astype(x.dtype)

def moba_attention(q, k, v):
    B, H, S, Dh = q.shape
    nb = -(-S // MOBA_BLOCK)
    pad = nb * MOBA_BLOCK - S
    kp = jnp.pad(k, ((0, 0), (0, 0), (0, pad), (0, 0)))
    vp = jnp.pad(v, ((0, 0), (0, 0), (0, pad), (0, 0)))
    kb = kp.reshape(B, H, nb, MOBA_BLOCK, Dh)
    vb = vp.reshape(B, H, nb, MOBA_BLOCK, Dh)
    slopes = _alibi_slopes(H)
    scale = HEAD_DIM ** -0.5

    counts = jnp.asarray(np.clip(S - np.arange(nb) * MOBA_BLOCK, 1, MOBA_BLOCK), dtype=jnp.float32)
    kmean = kb.astype(jnp.float32).sum(axis=3) / counts[:, None]
    pos = jnp.arange(S)
    qblk = pos // MOBA_BLOCK
    gate = jnp.einsum('bhtd,bhnd->bhtn', q.astype(jnp.float32), kmean)
    past = jnp.arange(nb)[None, :] < qblk[:, None]
    gate = jnp.where(past[None, None], gate, -jnp.inf)
    n_sel = max(1, min(MOBA_TOPK, nb - 1))
    _, sel = lax.top_k(gate, n_sel)
    sel_valid = jnp.arange(n_sel)[None, :] < qblk[:, None]

    nc = S // QUERY_CHUNK
    qc = q.reshape(B, H, nc, QUERY_CHUNK, Dh).transpose(2, 0, 1, 3, 4)
    selc = sel.reshape(B, H, nc, QUERY_CHUNK, n_sel).transpose(2, 0, 1, 3, 4)
    validc = sel_valid.reshape(nc, QUERY_CHUNK, n_sel)
    bi = jnp.arange(B)[:, None, None, None]
    hi = jnp.arange(H)[None, :, None, None]
    blk_off = jnp.arange(MOBA_BLOCK)

    def chunk(args):
        c, q_c, sel_c, valid_c = args
        t = c * QUERY_CHUNK + jnp.arange(QUERY_CHUNK)
        own = t[0] // MOBA_BLOCK
        k_own = lax.dynamic_index_in_dim(kb, own, axis=2, keepdims=False)
        v_own = lax.dynamic_index_in_dim(vb, own, axis=2, keepdims=False)
        s_own = own * MOBA_BLOCK + blk_off
        sc_own = jnp.einsum('bhtd,bhsd->bhts', q_c, k_own).astype(jnp.float32) * scale
        dist_own = (t[:, None] - s_own[None, :]).astype(jnp.float32)
        sc_own = sc_own - slopes[:, None, None] * dist_own[None]
        sc_own = jnp.where((s_own[None, :] <= t[:, None])[None, None], sc_own, -jnp.inf)

        k_sel = kb[bi, hi, sel_c]
        v_sel = vb[bi, hi, sel_c]
        s_sel = sel_c[..., None] * MOBA_BLOCK + blk_off
        sc_sel = jnp.einsum('bhtd,bhtrsd->bhtrs', q_c, k_sel).astype(jnp.float32) * scale
        dist_sel = (t[None, None, :, None, None] - s_sel).astype(jnp.float32)
        sc_sel = sc_sel - slopes[None, :, None, None, None] * dist_sel
        sc_sel = jnp.where(valid_c[None, None, :, :, None], sc_sel, -jnp.inf)

        scores = jnp.concatenate(
            [sc_own, sc_sel.reshape(B, H, QUERY_CHUNK, n_sel * MOBA_BLOCK)], axis=-1)
        p = jax.nn.softmax(scores, axis=-1)
        p_own = p[..., :MOBA_BLOCK].astype(v.dtype)
        p_sel = p[..., MOBA_BLOCK:].reshape(B, H, QUERY_CHUNK, n_sel, MOBA_BLOCK).astype(v.dtype)
        out = (jnp.einsum('bhts,bhsd->bhtd', p_own, v_own)
               + jnp.einsum('bhtrs,bhtrsd->bhtd', p_sel, v_sel))
        return out.astype(q.dtype)

    out = lax.map(chunk, (jnp.arange(nc), qc, selc, validc))
    return out.transpose(1, 2, 0, 3, 4).reshape(B, H, S, Dh)

def multiscale_pool(u, w_pool, pool_scale):
    B, S, _ = u.shape
    ug = u.astype(jnp.float32).reshape(B, S, N_POOL_GROUPS, POOL_GROUP)
    cs = jnp.cumsum(ug, axis=1)
    pos = jnp.arange(S)
    outs = []
    for g, w in enumerate(POOL_WINDOWS):
        c = cs[:, :, g]
        prev = jnp.pad(c, ((0, 0), (w, 0), (0, 0)))[:, :S]
        cnt = jnp.minimum(pos + 1, w).astype(jnp.float32)[None, :, None]
        outs.append((c - prev) / cnt - ug[:, :, g])
    mixed = jnp.stack(outs, axis=2)
    y = jnp.einsum('bsgc,gcd->bsgd', mixed, w_pool.astype(jnp.float32))
    y = y.reshape(B, S, POOL_WIDTH) * pool_scale.astype(jnp.float32)
    return y.astype(u.dtype)

def second_inputs(seed: int = 0) -> dict:
    key = jax.random.key(seed)
    ks = jax.random.split(key, 12)
    f32 = jnp.float32
    x = jax.random.normal(ks[0], (BATCH, SEQ, D_MODEL), f32)
    norm_mix = 1.0 + 0.02 * jax.random.normal(ks[1], (DEPTH, D_MODEL), f32)
    w_in = jax.random.normal(ks[2], (DEPTH, D_MODEL, IN_WIDTH), f32) * D_MODEL ** -0.5
    w_pool = jax.random.normal(ks[3], (DEPTH, N_POOL_GROUPS, POOL_GROUP, POOL_GROUP), f32) * POOL_GROUP ** -0.5
    pool_scale = 1.0 + 0.02 * jax.random.normal(ks[4], (DEPTH, POOL_WIDTH), f32)
    w_out = jax.random.normal(ks[5], (DEPTH, D_MODEL, D_MODEL), f32) * D_MODEL ** -0.5
    norm_mlp = 1.0 + 0.02 * jax.random.normal(ks[6], (DEPTH, D_MODEL), f32)
    w_up = jax.random.normal(ks[7], (DEPTH, D_MODEL, D_FF_2), f32) * D_MODEL ** -0.5
    w_down = jax.random.normal(ks[8], (DEPTH, D_FF_2, D_MODEL), f32) * D_FF_2 ** -0.5
    norm_final = 1.0 + 0.02 * jax.random.normal(ks[9], (D_MODEL,), f32)
    return {"x": x, "norm_mix": norm_mix, "w_in": w_in, "w_pool": w_pool,
            "pool_scale": pool_scale, "w_out": w_out, "norm_mlp": norm_mlp,
            "w_up": w_up, "w_down": w_down, "norm_final": norm_final}

def second_block(x, norm_mix, w_in, w_pool, pool_scale, w_out, norm_mlp, w_up, w_down, norm_final):
    B, S, _ = x.shape
    for l in range(DEPTH):
        h = rms_norm(x, norm_mix[l])
        proj = h @ w_in[l]
        q, k, v, u = jnp.split(proj, [ATTN_WIDTH, 2 * ATTN_WIDTH, 3 * ATTN_WIDTH], axis=-1)
        to_heads = lambda t: t.reshape(B, S, N_ATTN_HEADS_2, HEAD_DIM).transpose(0, 2, 1, 3)
        a = moba_attention(to_heads(q), to_heads(k), to_heads(v))
        a = a.transpose(0, 2, 1, 3).reshape(B, S, ATTN_WIDTH)
        p = multiscale_pool(u, w_pool[l], pool_scale[l])
        x = x + jnp.concatenate([a, p], axis=-1) @ w_out[l]
        h = rms_norm(x, norm_mlp[l])
        x = x + jnp.square(jax.nn.relu(h @ w_up[l])) @ w_down[l]
    return rms_norm(x, norm_final)


def setup_inputs(seed=0):
    out = dict(first_inputs(seed))
    for name, value in second_inputs(seed + 1).items():
        if name != "x":
            out[name + "_2"] = value
    return out


def reference(
    x, norm_mix_pre, norm_mix_post, norm_ffn_pre, norm_ffn_post, w_in_first, w_in_rest,
    mu_shift, mu_shift_mv, attn_out_gain, decay_w0, decay_up, aaa_a0, aaa_up, mv_v0, mv_up,
    gate_up, k_k, k_a, r_k, gn_w, gn_b, w_out, w_ffn_up, w_ffn_down, norm_mix_2, w_in_2,
    w_pool_2, pool_scale_2, w_out_2, norm_mlp_2, w_up_2, w_down_2, norm_final_2,
):
    x = first_block(
        x, norm_mix_pre, norm_mix_post, norm_ffn_pre, norm_ffn_post, w_in_first, w_in_rest,
        mu_shift, mu_shift_mv, attn_out_gain, decay_w0, decay_up, aaa_a0, aaa_up, mv_v0, mv_up,
        gate_up, k_k, k_a, r_k, gn_w, gn_b, w_out, w_ffn_up, w_ffn_down,
    )
    return second_block(
        x, norm_mix_2, w_in_2, w_pool_2, pool_scale_2, w_out_2, norm_mlp_2, w_up_2, w_down_2,
        norm_final_2,
    )


_drawn_inputs = setup_inputs


def setup_inputs(seed=0):
    import zlib

    import numpy as np

    out = dict(_drawn_inputs(seed))
    spreads = {}
    factors = {'decay_up': 4.921,
     'aaa_a0': 3.62,
     'gn_w': 3.133,
     'gn_b': 8.0,
     'norm_mix_2': 7.107,
     'pool_scale_2': 21.851,
     'norm_mlp_2': 19.055,
     'norm_final_2': 7.401}
    for name, (base, spread) in spreads.items():
        noise = np.random.default_rng([zlib.crc32(name.encode()), seed]).standard_normal(out[name].shape)
        drawn = base * np.exp(spread * noise) if base else spread * noise
        out[name] = __import__('jax').numpy.asarray(drawn.astype(out[name].dtype))
    for name, factor in factors.items():
        out[name] = (out[name] * factor).astype(out[name].dtype)
    return out
```

```python
from contextlib import ExitStack

import numpy as np

import concourse.bass as bass
from concourse import mybir

F32 = mybir.dt.float32
F32R = mybir.dt.float32r
I32 = mybir.dt.int32
ALU = mybir.AluOpType
ACT = mybir.ActivationFunctionType
AX = mybir.AxisListType.X

P = 128
S = 512
TT = S // P
D = 1024
KT = D // P
H = 8
N = 64
HP = H // 2
F = 4 * D
HALF = F // 2
HT = HALF // P
CH = 64
NB = S // P
GW = 256
BIG = 1.0e30
RMS_EPS = 1e-6
GN_EPS = 64e-5
LORA0 = 3 * 512 + 3 * 512
EXP_MHALF = float(np.exp(-0.5))
LN2 = float(np.log(2.0))
LN32 = float(np.log(3.0) - np.log(2.0))

PAGE = {}


def page_rows():
    at = 0
    for name, n in (("norm_mix_pre", 8), ("norm_mix_post", 8), ("norm_ffn_pre", 8), ("norm_ffn_post", 8),
                    ("norm_mix_2", 8), ("norm_mlp_2", 8), ("norm_final_2", 8), ("mu", 12), ("mu_wa", 1),
                    ("mu_ag", 1), ("attn_out_gain", 4), ("decay_w0", 4), ("aaa_a0", 4), ("k_k", 4), ("k_a", 4),
                    ("r_k", 4), ("gn_w", 4), ("gn_b", 4), ("pool_scale_2", 4)):
        PAGE[name] = (at, n)
        at += n
    return at


PAGE_ROWS = page_rows()
LEVELS = (2, 4, 8, 16, 32)


def program(nc, a, out):
    with ExitStack() as ctx:
        def sem(name):
            return ctx.enter_context(nc.semaphore(name))

        def held(stack):
            return lambda name, shape, dt=F32: stack.enter_context(nc.sbuf_tensor(name, shape, dt))

        sb = held(ctx)
        xT = sb("xT", [P, KT, S])
        w_raw = sb("w_raw", [P, 2, KT, GW])
        w_hi = sb("w_hi", [P, 2, KT, GW], F32R)
        w_lo = sb("w_lo", [P, 2, KT, GW], F32R)
        page = sb("page", [P, P])
        par = sb("par", [P, P])
        ident = sb("ident", [P, P])
        ones = sb("ones", [P, P])
        ones64 = sb("ones64", [P, P])
        rstd = sb("rstd", [P, S])
        slopes = sb("slopes", [P, 2, HP, 2])
        delta = sb("delta", [P, S])
        lncount = sb("lncount", [P, S])
        hsq = sb("hsq", [P, 2, S])
        eps = sb("eps", [P, 2])
        tmp = sb("tmp", [P, 4, S])

        with ExitStack() as s:
            r = held(s)
            h_hi = r("h_hi", [P, KT, S], F32R)
            h_lo = r("h_lo", [P, KT, S], F32R)
        with ExitStack() as s:
            r = held(s)
            LA = r("LA", [P, HP, 2, 2, P])
            KA = r("KA", [P, HP, 2, 2, P])
            Tm = r("Tm", [P, H, P])
            Rm = r("Rm", [P, H, P])
            Qm = r("Qm", [P, H, P])
            Mt = r("Mt", [P, H, P])
        h_region = sb("h_region", [P, 2 * KT * S])
        with ExitStack() as s:
            r = held(s)
            a_hi = r("a_hi", [P, HT, S], F32R)
            a_lo = r("a_lo", [P, HT, S], F32R)
            yT = r("yT", [P, KT, S])
        with ExitStack() as s:
            r = held(s)
            qkT = r("qkT", [P, 2 * HP, S])
            Vn = r("Vn", [P, TT, 512])
            rkv = r("rkv", [P, 3 * HP, S])
            with ExitStack() as s2:
                r2 = held(s2)
                kap = r2("kap", [P, HP, S])
                bh = r2("bh", [P, HP, S])
                dC = r2("dC", [P, HP, S // CH])
                lmask = r2("lmask", [P, 1 + len(LEVELS), P])
                tri = r2("tri", [P, 2, P])
                with ExitStack() as s3:
                    r3 = held(s3)
                    zraw = r3("zraw", [P, 2, S + 1])
                    lora_up = r3("lora_up", [P, 3, 512])
                    xwa = r3("xwa", [P, S])
                    xag = r3("xag", [P, S])
                    starts = r3("starts", [P, S])
                with ExitStack() as s3:
                    r3 = held(s3)
                    KR = r3("KR", [P, HP, 2, P])
                    khb = r3("khb", [P, HP, P])
                    bhb = r3("bhb", [P, HP, P])
                    ktb = r3("ktb", [P, HP, P])
                    btb = r3("btb", [P, HP, P])
                    vb = r3("vb", [P, HP, P])
                    St = r3("St", [P, HP, P])
                    Sd = r3("Sd", [P, HP, P])
        with ExitStack() as s:
            r = held(s)
            r("below_attention", [P, 2 * HP * S + TT * 512])
            qs = r("qs", [P, S])
            ks = r("ks", [P, S])
            Z = r("Z", [P, 2, S])
            Pm = r("Pm", [P, 2, S])
            PT = r("PT", [P, 2, S])
            r("rwkv_out", [P, HP * S])
            On = r("On", [P, TT, 512])
            negmax = r("negmax", [P, 8])
            rowsum = r("rowsum", [P, 8])
            rinv = r("rinv", [P, 8])
            osq = r("osq", [P, TT])
            cent = r("cent", [P, S])
            upad = r("upad", [P, 2, 16 + S])
            uT = r("uT", [P, HP, S])
            wpool = r("wpool", [P, 4, P])
            rcnt = r("rcnt", [P, 4, S])
        with ExitStack() as s:
            r = held(s)
            xn = r("xn", [P, TT, D])
        bonus = xT[:, 0:HP, :]
        gT = xT[:, HP:2 * HP, :]
        Vt, GV, Gs, Un = (tmp[:, n, :] for n in range(4))
        eE, eD = xwa[:, :], xag[:, :]
        eI, lx, nrm = (lora_up[:, n, :] for n in range(3))
        ktn, btn = (hsq[:, n, :] for n in range(2))

        ps = ctx.enter_context(nc.psum_tensor("ps", [P, 8, S], F32))
        rk, vy = rkv[:, 0:2 * HP, :], rkv[:, 2 * HP:3 * HP, :]

        names = (
            "consts_built", "page_loaded", "page_turned", "par_ready", "lora_loaded", "wpool_loaded",
            "x_loaded", "x_turned", "x_ready", "sq_ready", "sq_used", "sd_ready", "rstd_ready", "hf_ready", "hhi_ready",
            "hlo_ready", "w_hi_ready", "w_lo_ready", "mm_done", "tile_evacuated", "shifted", "squared", "square_f32",
            "y_added", "lora_act", "lora_mm", "lora_evacuated", "kk_sq", "kk_ss", "kk_norm",
            "cum_ready", "lx_ready", "decays_ready", "kk_ready", "prep_pool",
            "bonus_in", "bonus_sum", "prep_done", "block_staged_pool", "block_staged_dve", "block_turned", "natural_ready",
            "gram_done", "gram_masked", "r0_ready", "t0_turned", "t_ready", "m_ready", "q_done", "q_ready", "dt_done",
            "t_updated", "t_turned", "r_ready", "inverse_ready", "gv_done", "gv_ready", "state_ready", "g_done", "g_ready",
            "u_done", "u_ready", "x_done", "y_done", "y_ready", "mean_done", "centred", "centred_sq", "var_done",
            "gn_sd", "gn_done", "pair_staged", "s_done", "z_ready", "max_ready", "p_ready", "p_turned", "pt_ready",
            "pv_done", "o_ready", "o_sq", "o_sd", "o_scaled", "o_turned", "mix_f32", "window_ready", "pooled",
            "pool_scaled", "out_f32", "out_turned", "out_ready", "stored",
        )
        sm = {n: sem(n) for n in names}
        w_in = [sem("w_in_even"), sem("w_in_odd")]
        blk = ctx.enter_context(nc.Block())

        def at(value, i=None, per=0):
            return value if i is None else i * per + value

        def cols(name, i=0, n=1):
            base = PAGE[name][0]
            if isinstance(i, int):
                return par[:, base + i:base + i + n]
            return par[:, bass.ds(i + base, n)]

        def block(t, i):
            return t.rearrange("p h (b t) -> p h b t", t=P)[:, :, i, :]

        def four(x, n=4):
            return x.unsqueeze(1).broadcast_to([P, n, P])

        G_LORA, G_RKV, G_QK1, G_V1, G_OUT1, G_FFN1 = 0, 1, 7, 11, 13, 17
        T_LORA, T_RKV, T_QK1, T_V1, T_OUT1, T_FFN1 = 0, 2, 14, 22, 26, 34
        G_U2, G_QK2, G_V2, G_OUT2, G_FFN2 = 49, 51, 55, 57, 61
        T_U2, T_QK2, T_V2, T_OUT2, T_FFN2 = 82, 86, 94, 98, 106
        N_MIX1, N_POST1, N_FFN1, N_FPOST1, N_MIX2, N_FFN2, N_FINAL = range(7)
        H_MIX1, H_OUT1, H_FFN1, H_MIX2, H_OUT2, H_FFN2 = (8 * n for n in range(6))
        X_LOAD1, X_LOAD2, X_MIX1, X_FFN1, X_MIX2, X_FFN2 = (8 * n for n in range(6))

        @blk.sync
        def _(sp):
            def load(g, src, i=None, per=0, n=GW):
                if not (i is None and g < 2):
                    sp.wait_ge(sm["w_lo_ready"], at(g - 1, i, per))
                sp.dma_start(w_raw[:, g % 2, :, 0:n], src.rearrange("(k p) n -> p k n", p=P))\
                    .then_inc(w_in[g % 2], 16)

            sp.dma_start(xn[:, :, :], a["x"][0].rearrange("(t p) d -> p t d", p=P)).then_inc(sm["x_loaded"], 16)
            for name, (row, n) in PAGE.items():
                if name.startswith("mu"):
                    start = {"mu": 0, "mu_wa": 1536, "mu_ag": 1568}[name]
                    src = a["mu_shift"][0, start:start + n * P].rearrange("(k p) -> k p", p=P)
                elif name == "norm_final_2":
                    src = a[name].rearrange("(k p) -> k p", p=P)
                elif name == "r_k":
                    src = a[name].rearrange("o h n -> (o h n)").rearrange("(k p) -> k p", p=P)
                else:
                    src = a[name][0].rearrange("(k p) -> k p", p=P)
                sp.dma_start(page[row:row + n, :], src).then_inc(sm["page_loaded"], 16)
            w1 = a["w_in_first"]
            load(G_LORA, w1[:, LORA0:LORA0 + 160], n=160)
            load(G_RKV, w1[:, 1536:1536 + GW])
            for m, src, row in ((0, "decay_up", 0), (1, "aaa_up", 32), (2, "gate_up", 32)):
                rows = a[src].shape[1]
                sp.wait_ge(sm["consts_built"], 2)
                sp.dma_start(lora_up[row:row + rows, m, :], a[src][0]).then_inc(sm["lora_loaded"], 16)
            load(G_RKV + 1, w1[:, 1536 + GW:1536 + 2 * GW])
            with sp.Fori(0, 2) as i:
                load(G_RKV + 2, w1[:, bass.ds(i * 512 + 2048, GW)], i, 2)
                load(G_RKV + 3, w1[:, bass.ds(i * 512 + 2048 + GW, GW)], i, 2)
            with sp.Fori(0, 2) as i:
                load(G_QK1, w1[:, bass.ds(i * 512, GW)], i, 2)
                load(G_QK1 + 1, w1[:, bass.ds(i * 512 + GW, GW)], i, 2)
            for c in range(2):
                load(G_V1 + c, w1[:, 1024 + c * GW:1024 + (c + 1) * GW])

            def load_out(g, w):
                with sp.Fori(0, 2) as i:
                    for c in range(2):
                        load(g + c, w[:, bass.ds(i * 512 + c * GW, GW)], i, 2)

            def load_ffn(g, up, down):
                for half in range(2):
                    with sp.Fori(0, HT // 4) as i:
                        for c in range(2):
                            load(g + c, up[:, bass.ds(i * 512 + half * HALF + c * GW, GW)], i, 2)
                    g += HT // 2
                    with sp.Fori(0, 2) as i:
                        for c in range(4):
                            rows = half * HALF + (c % 2) * D
                            load(g + c, down[rows:rows + D, bass.ds(i * 512 + (c // 2) * GW, GW)], i, 4)
                    g += 8

            load_out(G_OUT1, a["w_out"][0])
            sp.wait_ge(sm["hlo_ready"], H_OUT1 + 8)
            sp.dma_start(xn[:, :, :], a["x"][0].rearrange("(t p) d -> p t d", p=P)).then_inc(sm["x_loaded"], 16)
            load_ffn(G_FFN1, a["w_ffn_up"][0], a["w_ffn_down"][0])
            w2 = a["w_in_2"][0]
            for c in range(2):
                load(G_U2 + c, w2[:, 1536 + c * GW:1536 + (c + 1) * GW])
            with sp.Fori(0, 2) as i:
                for c in range(2):
                    load(G_QK2 + c, w2[:, bass.ds(i * 512 + c * GW, GW)], i, 2)
            for c in range(2):
                load(G_V2 + c, w2[:, 1024 + c * GW:1024 + (c + 1) * GW])
            load_out(G_OUT2, a["w_out_2"][0])
            load_ffn(G_FFN2, a["w_up_2"][0], a["w_down_2"][0])
            sp.wait_ge(sm["out_ready"], KT)
            sp.dma_start(out[0].rearrange("(t p) d -> p t d", p=P), xn[:, :, :]).then_inc(sm["stored"], 16)
            sp.wait_ge(sm["stored"], 16)

        @blk.tensor
        def _(pe):
            mm = nc.tensor.matmul

            def product(g, tile, banks, hb, hi, lo, first=True, last=True, i=None, per=0, tper=0, between=None):
                pe.wait_ge(sm["w_lo_ready"], at(g + 1, i, per))
                for j in range(2):
                    if first and not (i is None and tile + j < 4):
                        pe.wait_ge(sm["tile_evacuated"], at(tile + j - 3, i, tper))
                    o = ps[:, banks[j], :]
                    for k in range(KT):
                        whi = w_hi[:, g % 2, k, j * P:(j + 1) * P]
                        wlo = w_lo[:, g % 2, k, j * P:(j + 1) * P]
                        mm(o, whi, hi[:, hb + k, :], start=first and k == 0, stop=False)
                        mm(o, whi, lo[:, hb + k, :], start=False, stop=False)
                        m = mm(o, wlo, hi[:, hb + k, :], start=False, stop=last and k == KT - 1)
                    m.then_inc(sm["mm_done"], 1)
                    if between is not None and j == 0:
                        between()

            def product_loop(g, tile, n, between=None):
                with pe.Fori(0, n) as i:
                    for c in range(2):
                        product(g + c, tile + 2 * c, [(tile + 2 * c + j) % 4 for j in range(2)], 0, h_hi, h_lo,
                                i=i, per=2, tper=4, between=between and (lambda: between(i, c)))

            def product_natural(g, tile):
                for c in range(2):
                    pe.wait_ge(sm["w_lo_ready"], g + c + 1)
                    for b in range(2):
                        t = tile + 2 * c + b
                        pe.wait_ge(sm["tile_evacuated"], t - 3)
                        for q in range(2):
                            o = ps[:, t % 4, q * GW:(q + 1) * GW]
                            tok = slice((2 * b + q) * P, (2 * b + q + 1) * P)
                            for k in range(KT):
                                whi, wlo = w_hi[:, (g + c) % 2, k, :], w_lo[:, (g + c) % 2, k, :]
                                mm(o, h_hi[:, k, tok], whi, start=k == 0, stop=False)
                                mm(o, h_hi[:, k, tok], wlo, start=False, stop=False)
                                m = mm(o, h_lo[:, k, tok], whi, start=False, stop=k == KT - 1)
                        m.then_inc(sm["mm_done"], 1)

            def turn_x(load):
                pe.wait_ge(sm["x_loaded"], 16 * (load + 1))
                for k in range(KT):
                    if k >= 2:
                        pe.wait_ge(sm["x_ready"], 8 * load + k - 1)
                    for t in range(TT):
                        m = nc.tensor.transpose(ps[:, 4 + k % 2, t * P:(t + 1) * P], xn[:, t, k * P:(k + 1) * P], ident[:, :])
                    m.then_inc(sm["x_turned"], 1)

            def square_sums(n):
                for k in range(KT):
                    pe.wait_ge(sm["sq_ready"], 8 * n + k + 1)
                    mm(ps[:, 6, :], ones[:, :], hsq[:, k % 2, :], start=k == 0, stop=k == KT - 1)\
                        .then_inc(sm["sq_used"], 1)

            def ffn(g, tile, h):
                for half in range(2):
                    if half == 0:
                        for k in range(KT):
                            pe.wait_ge(sm["hlo_ready"], h + k + 1)
                    product_loop(g, tile, HT // 4)
                    g, tile = g + HT // 2, tile + HT
                    base = (0 if g < G_QK2 else 2 * HT) + half * HT
                    with pe.Fori(0, 2) as i:
                        for c in range(4):
                            if c < 2:
                                pe.wait_ge(sm["squared"], base + 8 * (c + 1) + 4)
                            product(g + c, tile + 2 * (c // 2), [(tile + 2 * (c // 2) + j) % 4 for j in range(2)],
                                    8 * (c % 2), a_hi, a_lo, first=c % 2 == 0, last=c % 2 == 1, i=i, per=4, tper=4)
                    g, tile = g + 8, tile + 8

            pe.wait_ge(sm["consts_built"], 1)
            pe.wait_ge(sm["page_loaded"], 16 * len(PAGE))
            nc.tensor.transpose(ps[:, 7, 0:PAGE_ROWS], page[0:PAGE_ROWS, :], ident[0:PAGE_ROWS, 0:PAGE_ROWS])\
                .then_inc(sm["page_turned"], 1)
            turn_x(0)
            square_sums(N_MIX1)
            pe.wait_ge(sm["w_lo_ready"], 1)
            for j in range(2):
                for k in range(KT):
                    if j == 0:
                        pe.wait_ge(sm["hlo_ready"], H_MIX1 + k + 1)
                    whi, wlo = (w[:, 0, k, 32 * j:32 * j + P] for w in (w_hi, w_lo))
                    mm(ps[:, j, :], whi, h_hi[:, k, :], start=k == 0, stop=False)
                    mm(ps[:, j, :], whi, h_lo[:, k, :], start=False, stop=False)
                    m = mm(ps[:, j, :], wlo, h_hi[:, k, :], start=False, stop=k == KT - 1)
                m.then_inc(sm["mm_done"], 1)
            for c in range(2):
                product(G_RKV + c, T_RKV + 2 * c, [(T_RKV + 2 * c + j) % 4 for j in range(2)], 0, h_hi, h_lo)
            pe.wait_ge(sm["lora_loaded"], 48)
            pe.wait_ge(sm["lora_act"], 1)
            for p in range(HP):
                if p:
                    pe.wait_ge(sm["lora_evacuated"], p)
                c = slice(p * P, (p + 1) * P)
                mm(ps[:, 4, :], lora_up[:, 0, c], xwa[:, :], start=True, stop=True)
                mm(ps[:, 5, :], lora_up[:, 1, c], xwa[:, :], start=True, stop=True)
                mm(ps[:, 6, :], lora_up[:, 2, c], xag[:, :], start=True, stop=True).then_inc(sm["lora_mm"], 1)
            product_loop(G_RKV + 2, T_RKV + 4, 2)

            def head_sums(i, c):
                pe.wait_ge(sm["kk_sq"], at(c + 1, i, 2))
                mm(ps[:, 7, :], ones64[:, :], hsq[:, 0, :], start=True, stop=True).then_inc(sm["kk_ss"], 1)
                pe.wait_ge(sm["bonus_in"], at(c + 1, i, 2))
                mm(ps[:, 6, :], ones64[:, :], tmp[:, 1, :], start=True, stop=True).then_inc(sm["bonus_sum"], 1)

            product_loop(G_QK1, T_QK1, 2, between=head_sums)
            product_natural(G_V1, T_V1)
            pe.wait_ge(sm["tile_evacuated"], T_OUT1)
            with pe.Fori(0, NB) as i:
                pe.wait_ge(sm["block_staged_pool"], at(1, i, 1))
                pe.wait_ge(sm["block_staged_dve"], at(1, i, 1))
                for n, src in enumerate((vb, ktb, btb)):
                    for p in range(HP):
                        m = nc.tensor.transpose(ps[:, n, p * P:(p + 1) * P], src[:, p, :], ident[:, :])
                    m.then_inc(sm["block_turned"], 1)
                for kind, src in enumerate((bhb, khb)):
                    for b in range(4):
                        e, g = b % 2, b // 2
                        if kind == 1:
                            pe.wait_ge(sm["gram_masked"], at(b + 1, i, 8))
                        for q in range(2):
                            p = 2 * g + q
                            m = mm(ps[:, 4 + b, q * 2 * P:(q + 1) * 2 * P], src[64 * e:64 * e + 64, p, :],
                                   KR[64 * e:64 * e + 64, p, :, :].rearrange("c a t -> c (a t)"), start=True, stop=True)
                        m.then_inc(sm["gram_done"], 1)
                pe.wait_ge(sm["natural_ready"], at(3, i, 3))
                for g in range(2):
                    pe.wait_ge(sm["r0_ready"], at(g + 1, i, 2))
                    for h in range(4 * g, 4 * g + 4):
                        m = nc.tensor.transpose(ps[:, 2 * g, (h % 4) * P:(h % 4 + 1) * P], Rm[:, h, :], ident[:, :])
                    m.then_inc(sm["t0_turned"], 1)
                pe.wait_ge(sm["gram_masked"], at(8, i, 8))
                for h in range(H):
                    m = mm(ps[:, 4, h * N:(h + 1) * N], KA[:, h // 2, h % 2, 0, :], Vt[:, h * N:(h + 1) * N], start=True, stop=True)
                m.then_inc(sm["gv_done"], 1)
                nl = len(LEVELS)
                for l in range(nl):
                    for g in range(2):
                        n = 2 * l + g
                        pe.wait_ge(sm["m_ready"], at(n + 1, i, 2 * nl))
                        if l == 0:
                            pe.wait_ge(sm["t_ready"], at(g + 1, i, 2))
                        else:
                            pe.wait_ge(sm["r_ready"], at(n - 1, i, 2 * nl - 2))
                        for h in range(4 * g, 4 * g + 4):
                            m = mm(ps[:, 2 * g, (h % 4) * P:(h % 4 + 1) * P], Mt[:, h, :], Tm[:, h, :], start=True, stop=True)
                        m.then_inc(sm["q_done"], 1)
                    for g in range(2):
                        n = 2 * l + g
                        pe.wait_ge(sm["q_ready"], at(n + 1, i, 2 * nl))
                        for h in range(4 * g, 4 * g + 4):
                            o = ps[:, 2 * g + 1, (h % 4) * P:(h % 4 + 1) * P]
                            if l < nl - 1:
                                m = mm(o, Rm[:, h, :], Qm[:, h, :], start=True, stop=True)
                            else:
                                m = mm(o, Qm[:, h, :], Rm[:, h, :], start=True, stop=True)
                        m.then_inc(sm["dt_done"], 1)
                    if l < nl - 1:
                        for g in range(2):
                            n = 2 * l + g
                            pe.wait_ge(sm["t_updated"], at(n + 1, i, 2 * nl - 2))
                            for h in range(4 * g, 4 * g + 4):
                                m = nc.tensor.transpose(ps[:, 2 * g, (h % 4) * P:(h % 4 + 1) * P], Tm[:, h, :], ident[:, :])
                            m.then_inc(sm["t_turned"], 1)
                pe.wait_ge(sm["gv_ready"], at(1, i, 1))
                pe.wait_ge(sm["inverse_ready"], at(2, i, 2))
                for c in range(2):
                    r = slice(c * CH, (c + 1) * CH)
                    pe.wait_ge(sm["state_ready"], at(c + 1, i, 2))
                    for p in range(HP):
                        m = mm(ps[r, 4, p * P:(p + 1) * P], KR[:, p, 0, r], St[:, p, :], start=True, stop=True)
                    m.then_inc(sm["g_done"], 1)
                    for p in range(HP):
                        mm(ps[:, 5, p * P + c * CH:p * P + (c + 1) * CH], St[:, p, :], KR[:, p, 1, r],
                           start=(c == 0 and p == 0), stop=False, skip_group_check=True)
                    pe.wait_ge(sm["g_ready"], at(c + 1, i, 2))
                    mm(ps[:, 7, 0:P], ktn[r, 0:P], Vt[r, 0:P], start=True, stop=False)
                    for h in range(H):
                        m = mm(ps[r, 6, h * N:(h + 1) * N], Rm[r, h, r], Gs[r, h * N:(h + 1) * N], start=True, stop=True)
                    m.then_inc(sm["u_done"], 1)
                    pe.wait_ge(sm["u_ready"], at(c + 1, i, 2))
                    for p in range(HP):
                        q = slice(p * P, (p + 1) * P)
                        if p:
                            mm(ps[:, 7, q], ktn[r, q], Vt[r, q], start=True, stop=False)
                        m = mm(ps[:, 7, q], btn[r, q], Un[r, q], start=False, stop=True)
                    m.then_inc(sm["x_done"], 1)
                for h in range(H):
                    p, e = h // 2, h % 2
                    o = ps[64 * e:64 * e + 64, 5, p * P:(p + 1) * P]
                    v = slice(h * N, (h + 1) * N)
                    mm(o, Vt[:, v], KA[:, p, e, 1, :], start=False, stop=False, skip_group_check=True)
                    m = mm(o, Un[:, v], LA[:, p, e, 1, :], start=False, stop=h == H - 1, skip_group_check=True)
                m.then_inc(sm["y_done"], 1)

            with pe.Fori(0, HP) as p:
                pe.wait_ge(sm["y_ready"], NB + 1)
                mm(ps[:, 4, :], ones64[:, :], vy[:, p, :], start=True, stop=True).then_inc(sm["mean_done"], 1)
                pe.wait_ge(sm["centred_sq"], at(1, p, 1))
                mm(ps[:, 5, :], ones64[:, :], hsq[:, 0, :], start=True, stop=True).then_inc(sm["var_done"], 1)

            def attention(b):
                def scores(n):
                    e, t = n // TT, n % TT
                    rows = slice(64 * e, 64 * e + 64)
                    mm(ps[:, 4 + n % 2, 0:(t + 1) * P], qs[rows, t * P:(t + 1) * P], ks[rows, 0:(t + 1) * P],
                       start=True, stop=True).then_inc(sm["s_done"], 1)

                with pe.Fori(0, HP) as i:
                    pe.wait_ge(sm["pair_staged"], at(4 * b + 1, i, 1))
                    scores(0)
                    for n in range(8):
                        e, t = n // TT, n % TT
                        if n < 7:
                            if n >= 1:
                                pass
                            scores(n + 1)
                        pe.wait_ge(sm["p_ready"], at(32 * b + n + 1, i, 8))
                        for j in range(t + 1):
                            m = nc.tensor.transpose(ps[:, 6 + n % 2, j * P:(j + 1) * P], Pm[:, n % 2, j * P:(j + 1) * P], ident[:, :])
                        m.then_inc(sm["p_turned"], 1)
                        if t == 0:
                            pe.wait_ge(sm["o_ready"], at(8 * b + e + 1, i, 2))
                        pe.wait_ge(sm["pt_ready"], at(32 * b + n + 1, i, 8))
                        for j in range(t + 1):
                            m = mm(ps[:, e, t * N:(t + 1) * N], PT[:, n % 2, j * P:(j + 1) * P],
                                   Vn[:, j, bass.ds(i * P + e * N, N)], start=j == 0, stop=j == t)
                        m.then_inc(sm["pv_done"], 1)
                for c in range(HP):
                    pe.wait_ge(sm["o_scaled"], TT * (b + 1))
                    if c >= 2:
                        pe.wait_ge(sm["mix_f32"], HP * b + c - 1)
                    for t in range(TT):
                        m = nc.tensor.transpose(ps[:, 4 + c % 2, t * P:(t + 1) * P], On[:, t, c * P:(c + 1) * P], ident[:, :])
                    m.then_inc(sm["o_turned"], 1)

            attention(0)
            for k in range(KT):
                pe.wait_ge(sm["hlo_ready"], H_OUT1 + k + 1)
            product_loop(G_OUT1, T_OUT1, 2)
            turn_x(1)
            square_sums(N_POST1)
            square_sums(N_FFN1)
            ffn(G_FFN1, T_FFN1, H_FFN1)
            square_sums(N_FPOST1)
            square_sums(N_MIX2)
            for k in range(KT):
                pe.wait_ge(sm["hlo_ready"], H_MIX2 + k + 1)
            for c in range(2):
                product(G_U2 + c, T_U2 + 2 * c, [(T_U2 + 2 * c + j) % 4 for j in range(2)], 0, h_hi, h_lo)
            product_loop(G_QK2, T_QK2, 2)
            product_natural(G_V2, T_V2)
            pe.wait_ge(sm["wpool_loaded"], 16)
            for g in range(4):
                pe.wait_ge(sm["window_ready"], g + 1)
                if g >= 2:
                    pe.wait_ge(sm["pool_scaled"], g - 1)
                mm(ps[:, 6 + g % 2, :], wpool[:, g, :], uT[:, g, :], start=True, stop=True).then_inc(sm["pooled"], 1)
            pe.wait_ge(sm["pool_scaled"], 4)
            attention(1)
            for k in range(KT):
                pe.wait_ge(sm["hlo_ready"], H_OUT2 + k + 1)
            product_loop(G_OUT2, T_OUT2, 2)
            square_sums(N_FFN2)
            ffn(G_FFN2, T_FFN2, H_FFN2)
            square_sums(N_FINAL)
            for k in range(KT):
                pe.wait_ge(sm["out_f32"], k + 1)
                if k >= 2:
                    pe.wait_ge(sm["out_ready"], k - 1)
                for t in range(TT):
                    m = nc.tensor.transpose(ps[:, 4 + k % 2, t * P:(t + 1) * P], tmp[:, k % 4, t * P:(t + 1) * P], ident[:, :])
                m.then_inc(sm["out_turned"], 1)

        @blk.scalar
        def _(act):
            af = nc.scalar.activation

            def split(g, i=None, per=0, n=GW):
                act.wait_ge(w_in[g % 2], at(16 * (g // 2 + 1), i, 8 * per))
                if not (i is None and g < 2):
                    act.wait_ge(sm["mm_done"], at(2 * (g - 1), i, 2 * per))
                af(w_hi[:, g % 2, :, 0:n], w_raw[:, g % 2, :, 0:n], ACT.Copy).then_inc(sm["w_hi_ready"], 1)

            def evacuate(g, j, tile, dst, i=None, per=0, func=ACT.Copy):
                act.wait_ge(sm["mm_done"], at(2 * g + j + 1, i, 2 * per))
                af(dst, ps[:, tile % 4, :], func).then_inc(sm["tile_evacuated"], 1)

            def turned_x(load):
                for k in range(KT):
                    act.wait_ge(sm["x_turned"], 8 * load + k + 1)
                    af(xT[:, k, :], ps[:, 4 + k % 2, :], ACT.Copy).then_inc(sm["x_ready"], 1)

            def squares(n, src, ready, base):
                for k in range(KT):
                    act.wait_ge(sm[ready], base + k + 1)
                    if 8 * n + k >= 2:
                        act.wait_ge(sm["sq_used"], 8 * n + k - 1)
                    af(hsq[:, k % 2, :], src[:, k, :], ACT.Square).then_inc(sm["sq_ready"], 1)
                act.wait_ge(sm["sq_used"], 8 * n + 8)
                af(rstd[:, :], ps[:, 6, :], ACT.Sqrt, bias=eps[:, 0:1], scale=1.0 / D).then_inc(sm["sd_ready"], 1)

            def upper(n):
                for k in range(KT):
                    act.wait_ge(sm["hf_ready"], KT * n + k + 1)
                    af(h_hi[:, k, :], tmp[:, k % 4, :], ACT.Copy).then_inc(sm["hhi_ready"], 1)

            def ffn(g, tile, b):
                for half in range(2):
                    with act.Fori(0, HT // 4) as i:
                        for c in range(2):
                            split(g + c + 1, i, 2)
                            for j in range(2):
                                m = 2 * c + j
                                n = (2 * b + half) * HT + m
                                act.wait_ge(sm["squared"], at(n + 1, i, 4))
                                evacuate(g + c, j, tile + m, tmp[:, m, :], i, 2, ACT.Relu)
                    g, tile = g + HT // 2, tile + HT

                    def down(c0, i, last=False):
                        for c in range(4):
                            if not (last and c == 3):
                                split(g + c0 + c + 1, i, 4)
                            if c % 2:
                                for j in range(2):
                                    m = 2 * (c // 2) + j
                                    evacuate(g + c0 + c, j, tile + c0 + m, tmp[:, m, :], i, 4)

                    if b == 1 and half == 1:
                        down(0, None)
                        down(4, None, last=True)
                    else:
                        with act.Fori(0, 2) as i:
                            down(0, i)
                    g, tile = g + 8, tile + 8

            act.wait_ge(sm["page_turned"], 1)
            af(par[:, 0:PAGE_ROWS], ps[:, 7, 0:PAGE_ROWS], ACT.Copy).then_inc(sm["par_ready"], 1)
            turned_x(0)
            split(G_LORA, n=160)
            act.wait_ge(sm["consts_built"], 1)
            squares(N_MIX1, xT, "x_ready", X_LOAD1)
            upper(0)
            split(G_RKV)
            for j in range(2):
                act.wait_ge(sm["mm_done"], j + 1)
                act.wait_ge(sm["consts_built"], 2)
                af(zraw[:, j, 1:S + 1], ps[:, j, :], ACT.Copy).then_inc(sm["tile_evacuated"], 1)
            act.wait_ge(sm["shifted"], 2)
            def rkv_tiles(g, tile, i=None):
                for c in range(2):
                    split(g + c + 1, i, 2)
                    for j in range(2):
                        m = 2 * c + j
                        act.wait_ge(sm["shifted"], at(tile + m - 1, i, 4))
                        evacuate(g + c, j, tile + m, zraw[:, m % 2, 1:S + 1], i, 2)

            rkv_tiles(G_RKV, T_RKV)
            af(xwa[0:32, :], xwa[0:32, :], ACT.Tanh)
            af(xag[:, :], xag[:, :], ACT.Sigmoid).then_inc(sm["lora_act"], 1)
            with act.Fori(0, HP) as p:
                act.wait_ge(sm["lora_mm"], at(1, p, 1))
                af(kap[:, p, :], ps[:, 4, :], ACT.Sigmoid, bias=cols("decay_w0", p))
                af(bh[:, p, :], ps[:, 5, :], ACT.Sigmoid, bias=cols("aaa_a0", p))
                af(gT[:, p, :], ps[:, 6, :], ACT.Copy).then_inc(sm["lora_evacuated"], 1)
            with act.Fori(0, 2) as i:
                rkv_tiles(G_RKV + 2, T_RKV + 4, i)

            def qk(g, tile, rwkv=False):
                with act.Fori(0, 2) as i:
                    for c in range(2):
                        split(g + c + 1, i, 2)
                        if rwkv:
                            act.wait_ge(sm["prep_done"], at(c + 1, i, 2))
                            act.wait_ge(sm["prep_pool"], at(c + 1, i, 2))
                            af(tmp[:, 0, :], rk[:, i * 2 + HP + c, :], ACT.Copy, scale=cols("k_k", i * 2 + c))
                            act.drain()
                            af(hsq[:, 0, :], tmp[:, 0, :], ACT.Square).then_inc(sm["kk_sq"], 1)
                            act.wait_ge(sm["cum_ready"], at(c + 1, i, 2))
                            af(eD, tmp[:, 3, :], ACT.Exp, scale=-EXP_MHALF)
                            af(eI, tmp[:, 3, :], ACT.Exp, scale=EXP_MHALF)
                            act.wait_ge(sm["lx_ready"], at(c + 1, i, 2))
                            af(eE, lx, ACT.Exp, scale=-EXP_MHALF).then_inc(sm["decays_ready"], 1)
                            act.wait_ge(sm["kk_ss"], at(c + 1, i, 2))
                            af(nrm, ps[:, 7, :], ACT.Sqrt).then_inc(sm["kk_norm"], 1)
                        for j in range(2):
                            m = 2 * c + j
                            evacuate(g + c, j, tile + m, qkT[:, i * 4 + m, :], i, 2)

            def natural_v(g, tile):
                for c in range(2):
                    split(g + c + 1)
                    for b in range(2):
                        act.wait_ge(sm["mm_done"], 2 * (g + c) + b + 1)
                        af(Vn[:, 2 * b:2 * b + 2, c * GW:(c + 1) * GW],
                           ps[:, (tile + 2 * c + b) % 4, :].rearrange("p (t n) -> p t n", t=2), ACT.Copy)\
                            .then_inc(sm["tile_evacuated"], 1)

            qk(G_QK1, T_QK1, rwkv=True)
            natural_v(G_V1, T_V1)
            nl = len(LEVELS)
            with act.Fori(0, NB) as i:
                for n, dst in enumerate((Vt, ktn, btn)):
                    act.wait_ge(sm["block_turned"], at(n + 1, i, 3))
                    af(dst, ps[:, n, :], ACT.Copy).then_inc(sm["natural_ready"], 1)
                for g in range(2):
                    act.wait_ge(sm["t0_turned"], at(g + 1, i, 2))
                    af(Tm[:, 4 * g:4 * g + 4, :], ps[:, 2 * g, :].rearrange("p (h t) -> p h t", t=P), ACT.Copy)\
                        .then_inc(sm["t_ready"], 1)
                act.wait_ge(sm["gv_done"], at(1, i, 1))
                af(GV, ps[:, 4, :], ACT.Copy).then_inc(sm["gv_ready"], 1)
                for l in range(nl):
                    for g in range(2):
                        act.wait_ge(sm["q_done"], at(2 * l + g + 1, i, 2 * nl))
                        af(Qm[:, 4 * g:4 * g + 4, :], ps[:, 2 * g, :].rearrange("p (h t) -> p h t", t=P), ACT.Copy)\
                            .then_inc(sm["q_ready"], 1)
                    if l < nl - 1:
                        for g in range(2):
                            act.wait_ge(sm["t_turned"], at(2 * l + g + 1, i, 2 * nl - 2))
                            af(Rm[:, 4 * g:4 * g + 4, :], ps[:, 2 * g, :].rearrange("p (h t) -> p h t", t=P), ACT.Copy)\
                                .then_inc(sm["r_ready"], 1)
                for c in range(2):
                    r = slice(c * CH, (c + 1) * CH)
                    act.wait_ge(sm["u_done"], at(c + 1, i, 2))
                    af(Un[r, :], ps[r, 6, :], ACT.Copy, scale=-1.0).then_inc(sm["u_ready"], 1)
                act.wait_ge(sm["y_done"], at(1, i, 1))
                af(block(vy, i), ps[:, 5, :].rearrange("p (h t) -> p h t", t=P), ACT.Copy).then_inc(sm["y_ready"], 1)
            with act.Fori(0, HP) as p:
                act.wait_ge(sm["centred"], at(1, p, 1))
                af(hsq[:, 0, :], cent[:, :], ACT.Square).then_inc(sm["centred_sq"], 1)
                act.wait_ge(sm["var_done"], at(1, p, 1))
                af(hsq[:, 1, :], ps[:, 5, :], ACT.Sqrt, bias=eps[:, 1:2], scale=1.0 / N).then_inc(sm["gn_sd"], 1)

            def attention(b):
                with act.Fori(0, HP) as i:
                    af(qs[:, :], qkT[:, i, :], ACT.Copy, scale=N ** -0.5)
                    af(ks[:, :], qkT[:, i + HP, :], ACT.Copy).then_inc(sm["pair_staged"], 1)
                    for n in range(8):
                        t = n % TT
                        act.wait_ge(sm["max_ready"], at(32 * b + n + 1, i, 8))
                        af(Pm[:, n % 2, 0:(t + 1) * P], Z[:, n % 2, 0:(t + 1) * P], ACT.Exp, bias=negmax[:, n:n + 1],
                           scale=-1.0, accum_out=rowsum[:, n:n + 1]).then_inc(sm["p_ready"], 1)
                        act.wait_ge(sm["p_turned"], at(32 * b + n + 1, i, 8))
                        af(PT[:, n % 2, 0:(t + 1) * P], ps[:, 6 + n % 2, 0:(t + 1) * P], ACT.Copy).then_inc(sm["pt_ready"], 1)
                if b == 0:
                    act.wait_ge(sm["o_ready"], 8 + 2)
                    for t in range(TT):
                        if t >= 1:
                            act.drain()
                        af(cent[:, :], On[:, t, :], ACT.Square, accum_out=osq[:, t:t + 1]).then_inc(sm["o_sq"], 1)
                    act.drain()
                    af(osq[:, :], osq[:, :], ACT.Sqrt, bias=eps[:, 0:1], scale=1.0 / 512).then_inc(sm["o_sd"], 1)
                for c in range(HP):
                    act.wait_ge(sm["o_turned"], HP * b + c + 1)
                    if b == 0:
                        af(tmp[:, c, :], ps[:, 4 + c % 2, :], ACT.Copy, scale=cols("attn_out_gain", c)).then_inc(sm["mix_f32"], 1)
                    else:
                        af(tmp[:, c, :], ps[:, 4 + c % 2, :], ACT.Copy).then_inc(sm["mix_f32"], 1)
                    act.drain()
                    af(h_hi[:, c, :], tmp[:, c, :], ACT.Copy).then_inc(sm["hhi_ready"], 1)

            def second_half(src):
                for p in range(HP):
                    af(h_hi[:, HP + p, :], src[:, p, :], ACT.Copy).then_inc(sm["hhi_ready"], 1)

            def out_product(g, tile, b):
                with act.Fori(0, 2) as i:
                    for c in range(2):
                        split(g + c + 1, i, 2)
                        for j in range(2):
                            m = 2 * c + j
                            dst = yT[:, i * 4 + m, :] if b == 0 else tmp[:, m, :]
                            if b == 1:
                                act.wait_ge(sm["x_ready"], at(X_MIX2 + m - 3, i, 4))
                            evacuate(g + c, j, tile + m, dst, i, 2)

            attention(0)
            act.wait_ge(sm["gn_done"], HP)
            second_half(vy)
            out_product(G_OUT1, T_OUT1, 0)
            turned_x(1)
            squares(N_POST1, yT, "tile_evacuated", T_OUT1)
            squares(N_FFN1, xT, "x_ready", X_MIX1)
            upper(1)
            ffn(G_FFN1, T_FFN1, 0)
            squares(N_FPOST1, yT, "y_added", HT // 2)
            squares(N_MIX2, xT, "x_ready", X_FFN1)
            upper(2)
            for c in range(2):
                split(G_U2 + c + 1)
                for j in range(2):
                    evacuate(G_U2 + c, j, T_U2 + 2 * c + j, uT[:, 2 * c + j, :])
            qk(G_QK2, T_QK2)
            natural_v(G_V2, T_V2)
            for g in range(4):
                act.wait_ge(sm["pooled"], g + 1)
                af(uT[:, g, :], ps[:, 6 + g % 2, :], ACT.Copy, scale=cols("pool_scale_2", g)).then_inc(sm["pool_scaled"], 1)
            attention(1)
            second_half(uT)
            out_product(G_OUT2, T_OUT2, 1)
            squares(N_FFN2, xT, "x_ready", X_MIX2)
            upper(3)
            ffn(G_FFN2, T_FFN2, 1)
            squares(N_FINAL, xT, "x_ready", X_FFN2 + 8)
            for k in range(KT):
                act.wait_ge(sm["out_turned"], k + 1)
                af(xn[:, :, k * P:(k + 1) * P], ps[:, 4 + k % 2, :].rearrange("p (t n) -> p t n", t=TT), ACT.Copy)\
                    .then_inc(sm["out_ready"], 1)

        @blk.vector
        def _(dve):
            v = nc.vector

            def split(g, i=None, per=0, n=GW):
                dve.wait_ge(sm["w_hi_ready"], at(g + 1, i, per))
                v.tensor_tensor(w_lo[:, g % 2, :, 0:n], w_raw[:, g % 2, :, 0:n], w_hi[:, g % 2, :, 0:n].bitcast(F32),
                                ALU.subtract).then_inc(sm["w_lo_ready"], 1)

            def inverse_root(n):
                dve.wait_ge(sm["sd_ready"], n + 1)
                v.reciprocal(rstd[:, :], rstd[:, :]).then_inc(sm["rstd_ready"], 1)
                dve.drain()

            def lower(h, k, src):
                dve.wait_ge(sm["hhi_ready"], h + k + 1)
                v.tensor_tensor(h_lo[:, k, :], src, h_hi[:, k, :].bitcast(F32), ALU.subtract).then_inc(sm["hlo_ready"], 1)

            def normed(h, gain):
                for k in range(KT + 1):
                    if k < KT:
                        v.scalar_tensor_tensor(out=tmp[:, k % 4, :], in0=xT[:, k, :], scalar=cols(gain, k), in1=rstd[:, :],
                                               op0=ALU.mult, op1=ALU.mult).then_inc(sm["hf_ready"], 1)
                    if k >= 1:
                        lower(h, k - 1, tmp[:, (k - 1) % 4, :])

            def add_normed(gain):
                for k in range(KT):
                    v.scalar_tensor_tensor(out=tmp[:, k % 4, :], in0=yT[:, k, :], scalar=cols(gain, k), in1=rstd[:, :],
                                           op0=ALU.mult, op1=ALU.mult)
                    dve.drain()
                    v.tensor_tensor(xT[:, k, :], xT[:, k, :], tmp[:, k % 4, :], ALU.add).then_inc(sm["x_ready"], 1)
                dve.drain()

            def ffn(g, tile, b):
                for half in range(2):
                    with dve.Fori(0, HT // 4) as i:
                        for c in range(2):
                            split(g + c + 1, i, 2)
                            for j in range(2):
                                m = 2 * c + j
                                dve.wait_ge(sm["tile_evacuated"], at(tile + m + 1, i, 4))
                                v.tensor_tensor(a_hi[:, i * 4 + m, :], tmp[:, m, :], tmp[:, m, :], ALU.mult)
                            dve.drain()
                            for j in range(2):
                                m = 2 * c + j
                                dve.wait_ge(sm["square_f32"], at((2 * b + half) * HT + m + 1, i, 4))
                                v.tensor_tensor(a_lo[:, i * 4 + m, :], hsq[:, m % 2, :], a_hi[:, i * 4 + m, :].bitcast(F32),
                                                ALU.subtract).then_inc(sm["squared"], 1)
                    g, tile = g + HT // 2, tile + HT

                    def down(c0, i, last=False):
                        for c in range(4):
                            if not (last and c == 3):
                                split(g + c0 + c + 1, i, 4)
                            if c % 2:
                                for j in range(2):
                                    m = 2 * (c // 2) + j
                                    dve.wait_ge(sm["tile_evacuated"], at(tile + c0 + m + 1, i, 4))
                                    k = c0 + m if i is None else i * 4 + m
                                    acc = (yT if b == 0 else xT)[:, k, :]
                                    done = "y_added" if b == 0 else "x_ready"
                                    if b == 0 and half == 0:
                                        v.tensor_copy(acc, tmp[:, m, :]).then_inc(sm[done], 1)
                                    else:
                                        v.tensor_tensor(acc, acc, tmp[:, m, :], ALU.add).then_inc(sm[done], 1)

                    if b == 1 and half == 1:
                        down(0, None)
                        down(4, None, last=True)
                    else:
                        with dve.Fori(0, 2) as i:
                            down(0, i)
                    g, tile = g + 8, tile + 8

            dve.wait_ge(sm["consts_built"], 2)
            di = xwa[:, :].bitcast(I32)
            m4, m16, m128 = tmp[:, 0, :], tmp[:, 1, :], tmp[:, 2, :]
            v.tensor_scalar(tmp[:, 3, :].bitcast(I32), di, 3, None, ALU.bitwise_and)
            v.tensor_scalar(tmp[:, 2, :].bitcast(I32), di, 15, None, ALU.bitwise_and)
            dve.drain()
            v.tensor_scalar(m4, tmp[:, 3, :].bitcast(I32), 0.0, None, ALU.is_equal)
            v.tensor_scalar(m16, tmp[:, 2, :].bitcast(I32), 0.0, None, ALU.is_equal)
            dve.drain()
            v.tensor_scalar(m128, delta[:, :], 128.0, None, ALU.is_le)
            dve.drain()
            v.tensor_tensor(m4, m4, m16, ALU.add)
            dve.drain()
            v.tensor_tensor(m4, m4, m128, ALU.add)
            v.tensor_scalar(tmp[:, 3, :], delta[:, :], 0.0, None, ALU.is_ge)
            dve.drain()
            v.tensor_tensor(m4, m4, tmp[:, 3, :], ALU.mult)
            dve.drain()
            v.tensor_scalar(lncount[:, :], m4, 1.0, BIG, ALU.is_lt, ALU.mult)
            v.tensor_scalar(m16, m4, 2.0, -LN2, ALU.is_ge, ALU.mult)
            v.tensor_scalar(m128, m4, 3.0, -LN32, ALU.is_ge, ALU.mult)
            dve.drain()
            v.tensor_tensor(lncount[:, :], lncount[:, :], m16, ALU.add)
            v.tensor_scalar(tmp[:, 3, :], delta[:, :], 0.0, BIG, ALU.is_lt, ALU.mult)
            dve.drain()
            v.tensor_tensor(lncount[:, :], lncount[:, :], m128, ALU.add)
            v.tensor_tensor(delta[:, :], delta[:, :], tmp[:, 3, :], ALU.add)
            dve.drain()

            split(G_LORA, n=160)
            inverse_root(N_MIX1)
            dve.wait_ge(sm["par_ready"], 1)
            normed(H_MIX1, "norm_mix_pre")
            split(G_RKV)

            def shift(slot, dst, mu):
                v.tensor_tensor(tmp[:, slot, :], zraw[:, slot, 0:S], zraw[:, slot, 1:S + 1], ALU.subtract)
                dve.drain()
                v.scalar_tensor_tensor(out=dst, in0=tmp[:, slot, :], scalar=mu, in1=zraw[:, slot, 1:S + 1],
                                       op0=ALU.mult, op1=ALU.add).then_inc(sm["shifted"], 1)

            for j, (dst, mu) in enumerate(((xwa, "mu_wa"), (xag, "mu_ag"))):
                dve.wait_ge(sm["tile_evacuated"], j + 1)
                shift(j, dst[:, :], cols(mu))
            with dve.Fori(0, 3) as i:
                for c in range(2):
                    split(G_RKV + c + 1, i, 2)
                    for j in range(2):
                        m = 2 * c + j
                        dve.wait_ge(sm["tile_evacuated"], at(T_RKV + m + 1, i, 4))
                        shift(j, rkv[:, i * 4 + m, :], cols("mu", i * 4 + m))

            dve.drain()
            dve.nop().then_inc(sm["prep_done"], 1)
            with dve.Fori(0, 2) as i:
                for c in range(2):
                    p = i * 2 + c
                    k_, r_, v_ = rk[:, p + HP, :], rk[:, p, :], vy[:, p, :]
                    split(G_QK1 + c + 1, i, 2)
                    dve.wait_ge(sm["prep_pool"], at(c + 1, i, 2))
                    v.tensor_tensor_scan(tmp[:, 3, :], starts[:, :], kap[:, p, :], 0.0, ALU.mult, ALU.add)\
                        .then_inc(sm["cum_ready"], 1)
                    v.tensor_scalar(tmp[:, 1, :], bh[:, p, :], -1.0, cols("k_a", p), ALU.add, ALU.mult)
                    dve.drain()
                    dve.wait_ge(sm["kk_sq"], at(c + 1, i, 2))
                    v.scalar_tensor_tensor(out=k_, in0=tmp[:, 1, :], scalar=1.0, in1=k_, op0=ALU.add, op1=ALU.mult)
                    dve.drain()
                    v.scalar_tensor_tensor(out=tmp[:, 1, :], in0=r_, scalar=cols("r_k", p), in1=k_, op0=ALU.mult, op1=ALU.mult)\
                        .then_inc(sm["bonus_in"], 1)
                    dve.wait_ge(sm["decays_ready"], at(c + 1, i, 2))
                    v.tensor_tensor(k_, k_, eI, ALU.mult)
                    v.tensor_copy(dC[:, p, :], eD[:, CH - 1:S:CH])
                    dve.wait_ge(sm["kk_norm"], at(c + 1, i, 2))
                    v.tensor_scalar(nrm, nrm, 1e-12, None, ALU.max)
                    dve.drain()
                    v.reciprocal(nrm, nrm)
                    dve.drain()
                    v.tensor_tensor(tmp[:, 2, :], tmp[:, 0, :], nrm, ALU.mult).then_inc(sm["kk_ready"], 1)
                    dve.wait_ge(sm["bonus_sum"], at(c + 1, i, 2))
                    v.tensor_tensor(bonus[:, p, :], ps[:, 6, :], v_, ALU.mult)
                    dve.drain()
                    v.tensor_tensor(kap[:, p, :], tmp[:, 2, :], eE, ALU.mult).then_inc(sm["prep_done"], 1)
            for c in range(2):
                split(G_V1 + c + 1)
            nl = len(LEVELS)
            with dve.Fori(0, NB) as i:
                dve.wait_ge(sm["y_ready"], at(1, i, 1))
                dve.wait_ge(sm["prep_pool"], HP + 1)
                for dst, src in ((khb, rk[:, HP:2 * HP, :]), (bhb, bh[:, :, :])):
                    v.tensor_copy(dst[:, :, :], block(src, i))
                dce = dC[:, :, bass.ds(i * 2, 2)].unsqueeze(3).broadcast_to([P, HP, 2, CH])
                dve.drain()
                for n, (dst, src) in enumerate(((ktb, khb), (btb, bhb))):
                    m = v.tensor_tensor(dst[:, :, :].rearrange("p h (c t) -> p h c t", t=CH),
                                        src[:, :, :].rearrange("p h (c t) -> p h c t", t=CH), dce, ALU.mult)
                m.then_inc(sm["block_staged_dve"], 1)
                for kind, dst in enumerate((LA, KA)):
                    for b in range(4):
                        e, g = b % 2, b // 2
                        dve.wait_ge(sm["gram_done"], at(4 * kind + b + 1, i, 8))
                        v.tensor_tensor(dst[:, 2 * g:2 * g + 2, e, :, :].rearrange("p h a t -> p h (a t)"),
                                        ps[:, 4 + b, :].rearrange("p (h t) -> p h t", h=2),
                                        tri[:, :, :].rearrange("p a t -> p (a t)").unsqueeze(1).broadcast_to([P, 2, 2 * P]),
                                        ALU.mult).then_inc(sm["gram_masked"], 1)
                for l in range(nl):
                    for g in range(2):
                        hs = slice(4 * g, 4 * g + 4)
                        dt = ps[:, 2 * g + 1, :].rearrange("p (h t) -> p h t", t=P)
                        dve.wait_ge(sm["dt_done"], at(2 * l + g + 1, i, 2 * nl))
                        if l < nl - 1:
                            v.tensor_tensor(Tm[:, hs, :], Tm[:, hs, :], dt, ALU.subtract).then_inc(sm["t_updated"], 1)
                        else:
                            v.tensor_tensor(Rm[:, hs, :], Rm[:, hs, :], dt, ALU.subtract).then_inc(sm["inverse_ready"], 1)
                for c in range(2):
                    r = slice(c * CH, (c + 1) * CH)
                    if c == 1:
                        dve.drain()
                    v.tensor_tensor(Sd[:, :, :], St[:, :, :], dC[:, :, bass.ds(i * 2 + c, 1)].broadcast_to([P, HP, P]), ALU.mult)
                    dve.wait_ge(sm["g_done"], at(c + 1, i, 2))
                    v.tensor_tensor(Gs[r, :], ps[r, 4, :], GV[r, :], ALU.add).then_inc(sm["g_ready"], 1)
                    xs = ps[:, 7, :].rearrange("p (h n) -> p h n", n=P)
                    dve.wait_ge(sm["x_done"], at(c + 1, i, 2))
                    for e in range(2):
                        q = slice(64 * e, 64 * e + 64)
                        m = v.tensor_tensor(St[q, :, q], Sd[q, :, q], xs[q, :, q], ALU.add)
                    m.then_inc(sm["state_ready"], 1)
            with dve.Fori(0, HP) as p:
                dve.drain()
                dve.wait_ge(sm["mean_done"], at(1, p, 1))
                v.scalar_tensor_tensor(out=cent[:, :], in0=ps[:, 4, :], scalar=-1.0 / N, in1=vy[:, p, :], op0=ALU.mult,
                                       op1=ALU.add).then_inc(sm["centred"], 1)
                dve.wait_ge(sm["gn_sd"], at(1, p, 1))
                v.reciprocal(hsq[:, 1, :], hsq[:, 1, :])
                dve.drain()
                v.tensor_tensor(cent[:, :], cent[:, :], hsq[:, 1, :], ALU.mult)
                dve.drain()
                v.tensor_scalar(cent[:, :], cent[:, :], cols("gn_w", p), cols("gn_b", p), ALU.mult, ALU.add)
                dve.drain()
                v.tensor_tensor(cent[:, :], cent[:, :], bonus[:, p, :], ALU.add)
                dve.drain()
                v.tensor_tensor(vy[:, p, :], cent[:, :], gT[:, p, :], ALU.mult).then_inc(sm["gn_done"], 1)
            dve.drain()

            def attention(b):
                bias = lncount if b == 0 else delta

                def output(i, e):
                    dve.wait_ge(sm["pv_done"], at(32 * b + 4 * e + 4, i, 8))
                    v.reciprocal(rinv[:, 4 * e:4 * e + 4], rowsum[:, 4 * e:4 * e + 4])
                    dve.drain()
                    v.tensor_tensor(On[:, :, bass.ds(i * P + e * N, N)], ps[:, e, 0:TT * N].rearrange("p (t n) -> p t n", n=N),
                                    rinv[:, 4 * e:4 * e + 4].unsqueeze(2).broadcast_to([P, TT, N]), ALU.mult)\
                        .then_inc(sm["o_ready"], 1)

                with dve.Fori(0, HP) as i:
                    for n in range(8):
                        e, t = n // TT, n % TT
                        w = (t + 1) * P
                        dve.wait_ge(sm["s_done"], at(32 * b + n + 1, i, 8))
                        v.scalar_tensor_tensor(out=Z[:, n % 2, 0:w], in0=bias[:, (TT - 1 - t) * P:S], scalar=slopes[:, b, i, e:e + 1],
                                               in1=ps[:, 4 + n % 2, 0:w], op0=ALU.mult, op1=ALU.subtract).then_inc(sm["z_ready"], 1)
                        dve.drain()
                        v.tensor_reduce(negmax[:, n:n + 1], Z[:, n % 2, 0:w], AX, ALU.min).then_inc(sm["max_ready"], 1)
                        if n == 5:
                            output(i, 0)
                    output(i, 1)
                dve.drain()
                if b == 0:
                    dve.wait_ge(sm["o_sd"], 1)
                    v.reciprocal(osq[:, :], osq[:, :])
                    dve.drain()
                for t in range(TT):
                    if b == 0:
                        v.tensor_scalar(On[:, t, :], On[:, t, :], osq[:, t:t + 1], None, ALU.mult).then_inc(sm["o_scaled"], 1)
                    else:
                        dve.nop().then_inc(sm["o_scaled"], 1)
                for c in range(HP):
                    lower(H_OUT1 if b == 0 else H_OUT2, c, tmp[:, c, :])

            def out_product(g, tile, b):
                with dve.Fori(0, 2) as i:
                    for c in range(2):
                        split(g + c + 1, i, 2)
                        if b == 1:
                            for j in range(2):
                                m = 2 * c + j
                                dve.wait_ge(sm["tile_evacuated"], at(tile + m + 1, i, 4))
                                v.tensor_tensor(xT[:, i * 4 + m, :], xT[:, i * 4 + m, :], tmp[:, m, :], ALU.add)\
                                    .then_inc(sm["x_ready"], 1)

            attention(0)
            for p in range(HP):
                lower(H_OUT1, HP + p, vy[:, p, :])
            out_product(G_OUT1, T_OUT1, 0)
            inverse_root(N_POST1)
            dve.wait_ge(sm["x_ready"], X_LOAD2 + 8)
            add_normed("norm_mix_post")
            inverse_root(N_FFN1)
            normed(H_FFN1, "norm_ffn_pre")
            ffn(G_FFN1, T_FFN1, 0)
            inverse_root(N_FPOST1)
            add_normed("norm_ffn_post")
            inverse_root(N_MIX2)
            normed(H_MIX2, "norm_mix_2")
            for c in range(2):
                split(G_U2 + c + 1)
            dve.wait_ge(sm["consts_built"], 3)
            v.reciprocal(rcnt[:, :, :], rcnt[:, :, :])
            v.memset(upad[:, :, 0:16], 0.0)
            for g in range(4):
                split(G_QK2 + g + 1)
                dve.wait_ge(sm["tile_evacuated"], T_U2 + g + 1)
                v.tensor_copy(upad[:, 0, 16:16 + S], uT[:, g, :])
                dve.drain()
                for s in range(g + 1):
                    src, dst = upad[:, s % 2, :], upad[:, (s + 1) % 2, :]
                    v.tensor_tensor(dst[:, 16:16 + S], src[:, 16:16 + S], src[:, 16 - 2 ** s:16 - 2 ** s + S], ALU.add)
                    dve.drain()
                v.tensor_tensor(upad[:, (g + 1) % 2, 16:16 + S], upad[:, (g + 1) % 2, 16:16 + S], rcnt[:, g, :], ALU.mult)
                dve.drain()
                v.tensor_tensor(uT[:, g, :], upad[:, (g + 1) % 2, 16:16 + S], uT[:, g, :], ALU.subtract)\
                    .then_inc(sm["window_ready"], 1)
                dve.drain()
            for c in range(2):
                split(G_V2 + c + 1)
            attention(1)
            for p in range(HP):
                lower(H_OUT2, HP + p, uT[:, p, :])
            out_product(G_OUT2, T_OUT2, 1)
            dve.drain()
            inverse_root(N_FFN2)
            normed(H_FFN2, "norm_mlp_2")
            ffn(G_FFN2, T_FFN2, 1)
            dve.drain()
            inverse_root(N_FINAL)
            for k in range(KT):
                if k >= 4:
                    dve.wait_ge(sm["out_turned"], k - 3)
                v.scalar_tensor_tensor(out=tmp[:, k % 4, :], in0=xT[:, k, :], scalar=cols("norm_final_2", k), in1=rstd[:, :],
                                       op0=ALU.mult, op1=ALU.mult).then_inc(sm["out_f32"], 1)

        @blk.gpsimd
        def _(pool):
            g_ = nc.gpsimd

            def block_diagonal(x, size):
                view = x.rearrange("p (b t) -> p b t", t=size)
                g_.affine_select(out=view, in_=view, compare_op=ALU.is_ge, fill=0.0, base=0,
                                 pattern=[[-size, P // size], [0, size]], channel_multiplier=1)
                pool.drain()
                g_.affine_select(out=view, in_=view, compare_op=ALU.is_ge, fill=0.0, base=size - 1,
                                 pattern=[[size, P // size], [0, size]], channel_multiplier=-1)
                pool.drain()

            g_.memset(ident[:, :], 0.0)
            g_.memset(ones[:, :], 1.0)
            g_.memset(ones64[:, :], 1.0)
            g_.memset(eps[:, 0:1], RMS_EPS)
            g_.memset(eps[:, 1:2], GN_EPS)
            pool.drain()
            g_.affine_select(out=ident[:, :], in_=ident[:, :], compare_op=ALU.not_equal, fill=1.0, base=0,
                             pattern=[[-1, P]], channel_multiplier=1)
            block_diagonal(ones64[:, :], N)
            g_.memset(slopes[:, 0, :, :], 1.0).then_inc(sm["consts_built"], 1)
            g_.memset(zraw[:, :, 0:1], 0.0)
            g_.memset(lora_up[:, :, :], 0.0)
            g_.iota(xwa[:, :].bitcast(I32), pattern=[[-1, S]], base=3 * P, channel_multiplier=1)
            pool.drain()
            g_.tensor_copy(delta[:, :], xwa[:, :].bitcast(I32))
            pool.drain()
            for h in range(H):
                g_.memset(slopes[:, 1, h // 2, h % 2:h % 2 + 1], float(2.0 ** (-8.0 * (h + 1) / H)))
            g_.memset(starts[:, :], 1.0)
            pool.drain()
            g_.memset(starts[:, 0:S:CH], 0.0).then_inc(sm["consts_built"], 1)
            g_.memset(lmask[:, :, :], 1.0)
            g_.memset(tri[:, :, :], 1.0)
            pool.drain()
            for l in range(1 + len(LEVELS)):
                block_diagonal(lmask[:, l, :], 2 ** (l + 1))
            for m in range(2):
                block_diagonal(tri[:, m, :], CH)
            g_.affine_select(out=tri[:, 0, :], in_=tri[:, 0, :], compare_op=ALU.is_gt, fill=0.0, base=0, pattern=[[1, P]],
                             channel_multiplier=-1)
            g_.affine_select(out=tri[:, 1, :], in_=tri[:, 1, :], compare_op=ALU.is_ge, fill=0.0, base=0, pattern=[[1, P]],
                             channel_multiplier=-1)
            pool.drain()
            for l in range(len(LEVELS), 0, -1):
                g_.tensor_tensor(lmask[:, l, :], lmask[:, l, :], lmask[:, l - 1, :], ALU.subtract)
                pool.drain()
            g_.tensor_tensor(lmask[:, 0, :], lmask[:, 0, :], ident[:, :], ALU.subtract)
            pool.drain()
            pool.nop().then_inc(sm["y_ready"], 1)
            pool.nop().then_inc(sm["o_ready"], 2)
            pool.nop().then_inc(sm["prep_pool"], 1)

            for p in range(HP):
                pool.wait_ge(sm["cum_ready"], p + 1)
                g_.tensor_tensor(lx, tmp[:, 3, :], kap[:, p, :], ALU.subtract).then_inc(sm["lx_ready"], 1)
                pool.wait_ge(sm["decays_ready"], p + 1)
                pool.wait_ge(sm["bonus_in"], p + 1)
                g_.tensor_tensor(rk[:, p, :], rk[:, p, :], eD, ALU.mult)
                g_.tensor_tensor(bh[:, p, :], bh[:, p, :], eI, ALU.mult)
                pool.drain()
                pool.wait_ge(sm["kk_ready"], p + 1)
                g_.tensor_tensor(bh[:, p, :], bh[:, p, :], tmp[:, 2, :], ALU.mult).then_inc(sm["prep_pool"], 1)
            pool.wait_ge(sm["prep_done"], HP + 1)
            g_.memset(St[:, :, :], 0.0).then_inc(sm["state_ready"], 1)
            nl = len(LEVELS)
            Lv = LA[:, :, :, :, :].rearrange("p h e a t -> p (h e) a t")
            with pool.Fori(0, NB) as i:
                pool.wait_ge(sm["y_ready"], at(1, i, 1))
                g_.tensor_copy(KR[:, :, 0, :], block(kap[:, :, :], i))
                g_.tensor_copy(KR[:, :, 1, :], block(rk[:, 0:HP, :], i))
                g_.tensor_copy(vb[:, :, :], block(vy, i)).then_inc(sm["block_staged_pool"], 1)
                for g in range(2):
                    hs = slice(4 * g, 4 * g + 4)
                    pool.wait_ge(sm["gram_masked"], at(2 * g + 2, i, 8))
                    g_.tensor_tensor(Mt[:, hs, :], Lv[:, hs, 0, :], four(lmask[:, 0, :]), ALU.mult)
                    pool.drain()
                    g_.tensor_tensor(Rm[:, hs, :], four(ident[:, :]), Mt[:, hs, :], ALU.subtract).then_inc(sm["r0_ready"], 1)
                for l in range(nl):
                    for g in range(2):
                        hs = slice(4 * g, 4 * g + 4)
                        if l == 0:
                            pool.drain()
                        else:
                            pool.wait_ge(sm["q_done"], at(2 * (l - 1) + g + 1, i, 2 * nl))
                        g_.tensor_tensor(Mt[:, hs, :], Lv[:, hs, 0, :], four(lmask[:, l + 1, :]), ALU.mult)\
                            .then_inc(sm["m_ready"], 1)

            def squares_f32(tile, b):
                for half in range(2):
                    with pool.Fori(0, HT // 4) as i:
                        for m in range(4):
                            n = (2 * b + half) * HT + m
                            pool.wait_ge(sm["tile_evacuated"], at(tile + m + 1, i, 4))
                            pool.wait_ge(sm["squared"], at(n + 3, i, 4))
                            g_.tensor_tensor(hsq[:, m % 2, :], tmp[:, m, :], tmp[:, m, :], ALU.mult)\
                                .then_inc(sm["square_f32"], 1)
                    tile += HT + 8

            pool.nop().then_inc(sm["squared"], 4)
            squares_f32(T_FFN1, 0)
            pool.wait_ge(sm["tile_evacuated"], T_U2 + 1)
            pool.dma_start(wpool[:, :, :], a["w_pool_2"][0].rearrange("g c d -> c g d")).then_inc(sm["wpool_loaded"], 16)
            g_.iota(upad[:, 0, 0:S].bitcast(I32), pattern=[[1, S]], base=1, channel_multiplier=0)
            pool.drain()
            for g in range(4):
                g_.tensor_copy(rcnt[:, g, :], upad[:, 0, 0:S].bitcast(I32))
            pool.drain()
            for g in range(4):
                m = g_.tensor_scalar(rcnt[:, g, :], rcnt[:, g, :], float(2 ** (g + 1)), None, ALU.min)
            m.then_inc(sm["consts_built"], 1)
            squares_f32(T_FFN2, 1)


_INS = ("x", "norm_mix_pre", "norm_mix_post", "norm_ffn_pre", "norm_ffn_post", "w_in_first", "mu_shift", "attn_out_gain",
        "decay_w0", "decay_up", "aaa_a0", "aaa_up", "gate_up", "k_k", "k_a", "r_k", "gn_w", "gn_b", "w_out", "w_ffn_up",
        "w_ffn_down", "norm_mix_2", "w_in_2", "w_pool_2", "pool_scale_2", "w_out_2", "norm_mlp_2", "w_up_2", "w_down_2",
        "norm_final_2")


def kernel(**inputs):
    import concourse.bacc as bacc
    from concourse.bass_utils import run_bass_kernel_spmd

    nc = bacc.Bacc("TRN2", target_bir_lowering=False, num_devices=1)
    arrays, handles = {}, {}
    for name in _INS:
        array = np.ascontiguousarray(inputs[name])
        arrays[name + "_dram"] = array
        handles[name] = nc.dram_tensor(name + "_dram", array.shape, mybir.dt.from_np(array.dtype), kind="ExternalInput").ap()
    out = nc.dram_tensor("out_dram", (1, S, D), F32, kind="ExternalOutput").ap()
    program(nc, handles, out)
    return run_bass_kernel_spmd(nc, [arrays], core_ids=[0]).results[0]["out_dram"]
```

```python
from contextlib import ExitStack

import numpy as np

import concourse.bass as bass
from concourse import mybir

F32 = mybir.dt.float32
F32R = mybir.dt.float32r
I32 = mybir.dt.int32
ALU = mybir.AluOpType
ACT = mybir.ActivationFunctionType
AX = mybir.AxisListType.X

P = 128
S = 512
TT = S // P
D = 1024
KT = D // P
H = 8
N = 64
HP = H // 2
F = 4 * D
HALF = F // 2
HT = HALF // P
CH = 64
NB = S // P
GW = 256
BIG = 1.0e30
RMS_EPS = 1e-6
GN_EPS = 64e-5
LORA0 = 3 * 512 + 3 * 512
EXP_MHALF = float(np.exp(-0.5))
LN2 = float(np.log(2.0))
LN32 = float(np.log(3.0) - np.log(2.0))

PAGE = {}


def page_rows():
    at = 0
    for name, n in (("norm_mix_pre", 8), ("norm_mix_post", 8), ("norm_ffn_pre", 8), ("norm_ffn_post", 8),
                    ("norm_mix_2", 8), ("norm_mlp_2", 8), ("norm_final_2", 8), ("mu", 12), ("mu_wa", 1),
                    ("mu_ag", 1), ("attn_out_gain", 4), ("decay_w0", 4), ("aaa_a0", 4), ("k_k", 4), ("k_a", 4),
                    ("r_k", 4), ("gn_w", 4), ("gn_b", 4), ("pool_scale_2", 4)):
        PAGE[name] = (at, n)
        at += n
    return at


PAGE_ROWS = page_rows()
LEVELS = (2, 4, 8, 16, 32)


def program(nc, a, out):
    with ExitStack() as ctx:
        def sem(name):
            return ctx.enter_context(nc.semaphore(name))

        def held(stack):
            return lambda name, shape, dt=F32: stack.enter_context(nc.sbuf_tensor(name, shape, dt))

        sb = held(ctx)
        xT = sb("xT", [P, KT, S])
        w_raw = sb("w_raw", [P, 2, KT, GW])
        w_hi = sb("w_hi", [P, 2, KT, GW], F32R)
        w_lo = sb("w_lo", [P, 2, KT, GW], F32R)
        page = sb("page", [P, P])
        par = sb("par", [P, P])
        ident = sb("ident", [P, P])
        ones = sb("ones", [P, P])
        ones64 = sb("ones64", [P, P])
        rstd = sb("rstd", [P, S])
        slopes = sb("slopes", [P, 2, HP, 2])
        delta = sb("delta", [P, S])
        lncount = sb("lncount", [P, S])
        hsq = sb("hsq", [P, 2, S])
        eps = sb("eps", [P, 3])
        tmp = sb("tmp", [P, 4, S])

        with ExitStack() as s:
            r = held(s)
            h_hi = r("h_hi", [P, KT, S], F32R)
            h_lo = r("h_lo", [P, KT, S], F32R)
        with ExitStack() as s:
            r = held(s)
            LA = r("LA", [P, HP, 2, 2, P])
            KA = r("KA", [P, HP, 2, 2, P])
            Tm = r("Tm", [P, H, P])
            Rm = r("Rm", [P, H, P])
            Qm = r("Qm", [P, H, P])
            Mt = r("Mt", [P, H, P])
        h_region = sb("h_region", [P, 2 * KT * S])
        with ExitStack() as s:
            r = held(s)
            a_hi = r("a_hi", [P, HT, S], F32R)
            a_lo = r("a_lo", [P, HT, S], F32R)
            yT = r("yT", [P, KT, S])
        with ExitStack() as s:
            r = held(s)
            qkT = r("qkT", [P, 2 * HP, S])
            Vn = r("Vn", [P, TT, 512])
            rkv = r("rkv", [P, 3 * HP, S])
            with ExitStack() as s2:
                r2 = held(s2)
                kap = r2("kap", [P, HP, S])
                bh = r2("bh", [P, HP, S])
                dC = r2("dC", [P, HP, S // CH])
                lmask = r2("lmask", [P, 1 + len(LEVELS), P])
                tri = r2("tri", [P, 2, P])
                with ExitStack() as s3:
                    r3 = held(s3)
                    zraw = r3("zraw", [P, 2, S + 1])
                    lora_up = r3("lora_up", [P, 3, 512])
                    xwa = r3("xwa", [P, S])
                    xag = r3("xag", [P, S])
                    starts = r3("starts", [P, S])
                with ExitStack() as s3:
                    r3 = held(s3)
                    KR = r3("KR", [P, HP, 2, P])
                    khb = r3("khb", [P, HP, P])
                    bhb = r3("bhb", [P, HP, P])
                    ktb = r3("ktb", [P, HP, P])
                    btb = r3("btb", [P, HP, P])
                    vb = r3("vb", [P, HP, P])
                    St = r3("St", [P, HP, P])
                    Sd = r3("Sd", [P, HP, P])
        with ExitStack() as s:
            r = held(s)
            r("below_attention", [P, 2 * HP * S + TT * 512])
            qs = r("qs", [P, S])
            ks0 = r("ks0", [P, S])
            Z = r("Z", [P, 2, S])
            Pm = r("Pm", [P, 2, S])
            PT = r("PT", [P, 2, S])
            r("rwkv_out", [P, HP * S])
            On = r("On", [P, TT, 512])
            negmax = r("negmax", [P, 8])
            rowsum = r("rowsum", [P, 8])
            rinv = r("rinv", [P, 8])
            osq = r("osq", [P, TT])
            ks1 = r("ks1", [P, S])
            upad = r("upad", [P, 2, 16 + S])
            uT = r("uT", [P, HP, S])
            wpool = r("wpool", [P, 4, P])
            rcnt = r("rcnt", [P, 4, S])
        with ExitStack() as s:
            r = held(s)
            xn = r("xn", [P, TT, D])
        bonus = xT[:, 0:HP, :]
        gT = xT[:, HP:2 * HP, :]
        Vt, GV, Gs, Un = (tmp[:, n, :] for n in range(4))
        eE, eD = xwa[:, :], xag[:, :]
        eI, lx, nrm = (lora_up[:, n, :] for n in range(3))
        ktn, btn = (hsq[:, n, :] for n in range(2))

        ps = ctx.enter_context(nc.psum_tensor("ps", [P, 8, S], F32))
        rk, vy = rkv[:, 0:2 * HP, :], rkv[:, 2 * HP:3 * HP, :]

        names = (
            "consts_built", "page_loaded", "page_turned", "par_ready", "lora_loaded", "wpool_loaded",
            "x_loaded", "x_turned", "x_ready", "sq_ready", "sq_used", "tiles_summed", "sum_made", "sd_ready", "rstd_ready", "hf_ready", "hhi_ready",
            "hlo_ready", "w_hi_ready", "w_lo_ready", "mm_done", "tile_evacuated", "shifted", "squared", "square_f32",
            "y_added", "lora_act", "lora_mm", "lora_evacuated", "kk_sq", "kk_ss", "kk_norm",
            "cum_ready", "lx_ready", "decays_ready", "kk_ready", "prep_pool",
            "bonus_in", "bonus_sum", "prep_done", "block_staged_pool", "block_staged_act", "block_staged_dve", "block_turned", "natural_ready",
            "gram_done", "gram_masked", "r0_ready", "t0_turned", "t_ready", "m_ready", "q_done", "q_ready", "dt_done",
            "t_updated", "t_turned", "r_ready", "inverse_ready", "gv_done", "gv_ready", "state_ready", "g_done", "g_ready",
            "u_done", "u_ready", "x_done", "y_done", "y_ready", "mean_done", "centred", "centred_sq", "var_done",
            "gn_sd", "gn_scaled", "gn_done", "pair_staged", "s_done", "z_ready", "max_ready", "p_ready", "p_turned", "pt_ready",
            "pv_done", "o_ready", "o_sq", "o_sd", "o_scaled", "o_turned", "mix_f32", "window_ready", "pooled",
            "pool_scaled", "out_f32", "out_turned", "out_ready", "stored",
        )
        sm = {n: sem(n) for n in names}
        w_in = [sem("w_in_even"), sem("w_in_odd")]
        blk = ctx.enter_context(nc.Block())

        def at(value, i=None, per=0):
            return value if i is None else i * per + value

        def cols(name, i=0, n=1):
            base = PAGE[name][0]
            if isinstance(i, int):
                return par[:, base + i:base + i + n]
            return par[:, bass.ds(i + base, n)]

        def block(t, i):
            return t.rearrange("p h (b t) -> p h b t", t=P)[:, :, i, :]

        def four(x, n=4):
            return x.unsqueeze(1).broadcast_to([P, n, P])

        G_LORA, G_RKV, G_QK1, G_V1, G_OUT1, G_FFN1 = 0, 1, 7, 11, 13, 17
        T_LORA, T_RKV, T_QK1, T_V1, T_OUT1, T_FFN1 = 0, 2, 14, 22, 26, 34
        G_U2, G_QK2, G_V2, G_OUT2, G_FFN2 = 49, 51, 55, 57, 61
        T_U2, T_QK2, T_V2, T_OUT2, T_FFN2 = 82, 86, 94, 98, 106
        N_MIX1, N_POST1, N_FFN1, N_FPOST1, N_MIX2, N_FFN2, N_FINAL = range(7)
        H_MIX1, H_OUT1, H_FFN1, H_MIX2, H_OUT2, H_FFN2 = (8 * n for n in range(6))
        X_LOAD1, X_LOAD2, X_MIX1, X_FFN1, X_MIX2, X_FFN2 = (8 * n for n in range(6))

        @blk.sync
        def _(sp):
            def load(g, src, i=None, per=0, n=GW):
                if not (i is None and g < 2):
                    sp.wait_ge(sm["w_lo_ready"], at(g - 1, i, per))
                sp.dma_start(w_raw[:, g % 2, :, 0:n], src.rearrange("(k p) n -> p k n", p=P))\
                    .then_inc(w_in[g % 2], 16)

            sp.dma_start(xn[:, :, :], a["x"][0].rearrange("(t p) d -> p t d", p=P)).then_inc(sm["x_loaded"], 16)
            for name, (row, n) in PAGE.items():
                if name.startswith("mu"):
                    start = {"mu": 0, "mu_wa": 1536, "mu_ag": 1568}[name]
                    src = a["mu_shift"][0, start:start + n * P].rearrange("(k p) -> k p", p=P)
                elif name == "norm_final_2":
                    src = a[name].rearrange("(k p) -> k p", p=P)
                elif name == "r_k":
                    src = a[name].rearrange("o h n -> (o h n)").rearrange("(k p) -> k p", p=P)
                else:
                    src = a[name][0].rearrange("(k p) -> k p", p=P)
                sp.dma_start(page[row:row + n, :], src).then_inc(sm["page_loaded"], 16)
            w1 = a["w_in_first"]
            load(G_LORA, w1[:, LORA0:LORA0 + 160], n=160)
            load(G_RKV, w1[:, 1536:1536 + GW])
            for m, src, row in ((0, "decay_up", 0), (1, "aaa_up", 32), (2, "gate_up", 32)):
                rows = a[src].shape[1]
                sp.wait_ge(sm["consts_built"], 2)
                sp.dma_start(lora_up[row:row + rows, m, :], a[src][0]).then_inc(sm["lora_loaded"], 16)
            load(G_RKV + 1, w1[:, 1536 + GW:1536 + 2 * GW])
            with sp.Fori(0, 2) as i:
                load(G_RKV + 2, w1[:, bass.ds(i * 512 + 2048, GW)], i, 2)
                load(G_RKV + 3, w1[:, bass.ds(i * 512 + 2048 + GW, GW)], i, 2)
            with sp.Fori(0, 2) as i:
                load(G_QK1, w1[:, bass.ds(i * 512, GW)], i, 2)
                load(G_QK1 + 1, w1[:, bass.ds(i * 512 + GW, GW)], i, 2)
            for c in range(2):
                load(G_V1 + c, w1[:, 1024 + c * GW:1024 + (c + 1) * GW])

            def load_out(g, w):
                with sp.Fori(0, 2) as i:
                    for c in range(2):
                        load(g + c, w[:, bass.ds(i * 512 + c * GW, GW)], i, 2)

            def load_ffn(g, up, down):
                for half in range(2):
                    with sp.Fori(0, HT // 4) as i:
                        for c in range(2):
                            load(g + c, up[:, bass.ds(i * 512 + half * HALF + c * GW, GW)], i, 2)
                    g += HT // 2
                    with sp.Fori(0, 2) as i:
                        for c in range(4):
                            rows = half * HALF + (c % 2) * D
                            load(g + c, down[rows:rows + D, bass.ds(i * 512 + (c // 2) * GW, GW)], i, 4)
                    g += 8

            load_out(G_OUT1, a["w_out"][0])
            sp.wait_ge(sm["hlo_ready"], H_OUT1 + 8)
            sp.dma_start(xn[:, :, :], a["x"][0].rearrange("(t p) d -> p t d", p=P)).then_inc(sm["x_loaded"], 16)
            load_ffn(G_FFN1, a["w_ffn_up"][0], a["w_ffn_down"][0])
            w2 = a["w_in_2"][0]
            for c in range(2):
                load(G_U2 + c, w2[:, 1536 + c * GW:1536 + (c + 1) * GW])
            with sp.Fori(0, 2) as i:
                for c in range(2):
                    load(G_QK2 + c, w2[:, bass.ds(i * 512 + c * GW, GW)], i, 2)
            for c in range(2):
                load(G_V2 + c, w2[:, 1024 + c * GW:1024 + (c + 1) * GW])
            load_out(G_OUT2, a["w_out_2"][0])
            load_ffn(G_FFN2, a["w_up_2"][0], a["w_down_2"][0])
            for half in range(2):
                c = slice(half * D // 2, (half + 1) * D // 2)
                sp.wait_ge(sm["out_ready"], KT // 2 * (half + 1))
                sp.dma_start(out[0].rearrange("(t p) d -> p t d", p=P)[:, :, c], xn[:, :, c]).then_inc(sm["stored"], 16)
            sp.wait_ge(sm["stored"], 32)

        @blk.tensor
        def _(pe):
            mm = nc.tensor.matmul

            def product(g, tile, banks, hb, hi, lo, first=True, last=True, i=None, per=0, tper=0, between=None,
                        lower=None):
                pe.wait_ge(sm["w_lo_ready"], at(g + 1, i, per))
                for j in range(2):
                    if first and not (i is None and tile + j < 4):
                        pe.wait_ge(sm["tile_evacuated"], at(tile + j - 3, i, tper))
                    o = ps[:, banks[j], :]
                    for k in range(KT):
                        if lower is not None and j == 0:
                            pe.wait_ge(sm["hlo_ready"], lower + k + 1)
                        whi = w_hi[:, g % 2, k, j * P:(j + 1) * P]
                        wlo = w_lo[:, g % 2, k, j * P:(j + 1) * P]
                        mm(o, whi, hi[:, hb + k, :], start=first and k == 0, stop=False)
                        mm(o, whi, lo[:, hb + k, :], start=False, stop=False)
                        m = mm(o, wlo, hi[:, hb + k, :], start=False, stop=last and k == KT - 1)
                    m.then_inc(sm["mm_done"], 1)
                    if between is not None and j == 0:
                        between()

            def product_loop(g, tile, n, between=None, lower=None):
                with pe.Fori(0, n) as i:
                    for c in range(2):
                        product(g + c, tile + 2 * c, [(tile + 2 * c + j) % 4 for j in range(2)], 0, h_hi, h_lo,
                                i=i, per=2, tper=4, between=between and (lambda: between(i, c)),
                                lower=lower if c == 0 else None)

            def product_natural(g, tile):
                for c in range(2):
                    pe.wait_ge(sm["w_lo_ready"], g + c + 1)
                    for b in range(2):
                        t = tile + 2 * c + b
                        pe.wait_ge(sm["tile_evacuated"], t - 3)
                        for q in range(2):
                            o = ps[:, t % 4, q * GW:(q + 1) * GW]
                            tok = slice((2 * b + q) * P, (2 * b + q + 1) * P)
                            for k in range(KT):
                                whi, wlo = w_hi[:, (g + c) % 2, k, :], w_lo[:, (g + c) % 2, k, :]
                                mm(o, h_hi[:, k, tok], whi, start=k == 0, stop=False)
                                mm(o, h_hi[:, k, tok], wlo, start=False, stop=False)
                                m = mm(o, h_lo[:, k, tok], whi, start=False, stop=k == KT - 1)
                        m.then_inc(sm["mm_done"], 1)

            def turn_x(load, tiles=range(KT)):
                pe.wait_ge(sm["x_loaded"], 16 * (load + 1))
                for k in tiles:
                    if k >= 2:
                        pe.wait_ge(sm["x_ready"], 8 * load + k - 1)
                    for t in range(TT):
                        m = nc.tensor.transpose(ps[:, 4 + k % 2, t * P:(t + 1) * P], xn[:, t, k * P:(k + 1) * P], ident[:, :])
                    m.then_inc(sm["x_turned"], 1)

            def square_sums(n):
                for k in range(KT):
                    pe.wait_ge(sm["sq_ready"], 8 * n + k + 1)
                    mm(ps[:, 6, :], ones[:, :], hsq[:, k % 2, :], start=k == 0, stop=k == KT - 1)\
                        .then_inc(sm["sq_used"], 1)

            def square_total(n):
                pe.wait_ge(sm["tiles_summed"], n + 1)
                mm(ps[:, 6, :], ones[:, :], hsq[:, 0, :], start=True, stop=True).then_inc(sm["sum_made"], 1)

            def ffn(g, tile, h):
                for half in range(2):
                    product_loop(g, tile, HT // 4, lower=h if half == 0 else None)
                    g, tile = g + HT // 2, tile + HT
                    base = (0 if g < G_QK2 else 2 * HT) + half * HT
                    with pe.Fori(0, 2) as i:
                        for c in range(4):
                            if c < 2:
                                pe.wait_ge(sm["squared"], base + 8 * (c + 1) + 4)
                            product(g + c, tile + 2 * (c // 2), [(tile + 2 * (c // 2) + j) % 4 for j in range(2)],
                                    8 * (c % 2), a_hi, a_lo, first=c % 2 == 0, last=c % 2 == 1, i=i, per=4, tper=4)
                    g, tile = g + 8, tile + 8

            pe.wait_ge(sm["consts_built"], 1)
            pe.wait_ge(sm["page_loaded"], 16 * len(PAGE))
            nc.tensor.transpose(ps[:, 7, 0:PAGE_ROWS], page[0:PAGE_ROWS, :], ident[0:PAGE_ROWS, 0:PAGE_ROWS])\
                .then_inc(sm["page_turned"], 1)
            turn_x(0)
            square_sums(0)
            pe.wait_ge(sm["w_lo_ready"], 1)
            for j in range(2):
                for k in range(KT):
                    if j == 0:
                        pe.wait_ge(sm["hlo_ready"], H_MIX1 + k + 1)
                    whi, wlo = (w[:, 0, k, 32 * j:32 * j + P] for w in (w_hi, w_lo))
                    mm(ps[:, j, :], whi, h_hi[:, k, :], start=k == 0, stop=False)
                    mm(ps[:, j, :], whi, h_lo[:, k, :], start=False, stop=False)
                    m = mm(ps[:, j, :], wlo, h_hi[:, k, :], start=False, stop=k == KT - 1)
                m.then_inc(sm["mm_done"], 1)
            for c in range(2):
                product(G_RKV + c, T_RKV + 2 * c, [(T_RKV + 2 * c + j) % 4 for j in range(2)], 0, h_hi, h_lo)
            pe.wait_ge(sm["lora_loaded"], 48)
            pe.wait_ge(sm["lora_act"], 1)
            for p in range(HP):
                if p:
                    pe.wait_ge(sm["lora_evacuated"], p)
                c = slice(p * P, (p + 1) * P)
                mm(ps[:, 4, :], lora_up[:, 0, c], xwa[:, :], start=True, stop=True)
                mm(ps[:, 5, :], lora_up[:, 1, c], xwa[:, :], start=True, stop=True)
                mm(ps[:, 6, :], lora_up[:, 2, c], xag[:, :], start=True, stop=True).then_inc(sm["lora_mm"], 1)
            product_loop(G_RKV + 2, T_RKV + 4, 2)

            def head_sums(i, c):
                pe.wait_ge(sm["kk_sq"], at(c + 1, i, 2))
                mm(ps[:, 7, :], ones64[:, :], hsq[:, 0, :], start=True, stop=True).then_inc(sm["kk_ss"], 1)
                pe.wait_ge(sm["bonus_in"], at(c + 1, i, 2))
                mm(ps[:, 6, :], ones64[:, :], tmp[:, 1, :], start=True, stop=True).then_inc(sm["bonus_sum"], 1)

            product_loop(G_QK1, T_QK1, 2, between=head_sums)
            product_natural(G_V1, T_V1)
            pe.wait_ge(sm["tile_evacuated"], T_OUT1)
            with pe.Fori(0, NB) as i:
                for n, src in enumerate((vb, ktb, btb)):
                    if n == 0:
                        pe.wait_ge(sm["block_staged_pool"], at(1, i, 3))
                    else:
                        pe.wait_ge(sm["block_staged_dve"], at(n, i, 2))
                    for p in range(HP):
                        m = nc.tensor.transpose(ps[:, n, p * P:(p + 1) * P], src[:, p, :], ident[:, :])
                    m.then_inc(sm["block_turned"], 1)
                pe.wait_ge(sm["block_staged_act"], at(1, i, 1))
                for kind, src in enumerate((bhb, khb)):
                    pe.wait_ge(sm["block_staged_pool"], at(kind + 2, i, 3))
                    for b in range(4):
                        e, g = b % 2, b // 2
                        if kind == 1:
                            pe.wait_ge(sm["gram_masked"], at(b + 1, i, 8))
                        for q in range(2):
                            p = 2 * g + q
                            m = mm(ps[:, 4 + b, q * 2 * P:(q + 1) * 2 * P], src[64 * e:64 * e + 64, p, :],
                                   KR[64 * e:64 * e + 64, p, :, :].rearrange("c a t -> c (a t)"), start=True, stop=True)
                        m.then_inc(sm["gram_done"], 1)
                pe.wait_ge(sm["natural_ready"], at(3, i, 3))
                for g in range(2):
                    pe.wait_ge(sm["r0_ready"], at(g + 1, i, 2))
                    for h in range(4 * g, 4 * g + 4):
                        m = nc.tensor.transpose(ps[:, 2 * g, (h % 4) * P:(h % 4 + 1) * P], Rm[:, h, :], ident[:, :])
                    m.then_inc(sm["t0_turned"], 1)
                pe.wait_ge(sm["gram_masked"], at(8, i, 8))
                for h in range(H):
                    m = mm(ps[:, 4, h * N:(h + 1) * N], KA[:, h // 2, h % 2, 0, :], Vt[:, h * N:(h + 1) * N], start=True, stop=True)
                m.then_inc(sm["gv_done"], 1)
                nl = len(LEVELS)
                for l in range(nl):
                    for g in range(2):
                        n = 2 * l + g
                        pe.wait_ge(sm["m_ready"], at(n + 1, i, 2 * nl))
                        if l == 0:
                            pe.wait_ge(sm["t_ready"], at(g + 1, i, 2))
                        else:
                            pe.wait_ge(sm["r_ready"], at(n - 1, i, 2 * nl - 2))
                        for h in range(4 * g, 4 * g + 4):
                            m = mm(ps[:, 2 * g, (h % 4) * P:(h % 4 + 1) * P], Mt[:, h, :], Tm[:, h, :], start=True, stop=True)
                        m.then_inc(sm["q_done"], 1)
                    for g in range(2):
                        n = 2 * l + g
                        pe.wait_ge(sm["q_ready"], at(n + 1, i, 2 * nl))
                        for h in range(4 * g, 4 * g + 4):
                            o = ps[:, 2 * g + 1, (h % 4) * P:(h % 4 + 1) * P]
                            if l < nl - 1:
                                m = mm(o, Rm[:, h, :], Qm[:, h, :], start=True, stop=True)
                            else:
                                m = mm(o, Qm[:, h, :], Rm[:, h, :], start=True, stop=True)
                        m.then_inc(sm["dt_done"], 1)
                    if l < nl - 1:
                        for g in range(2):
                            n = 2 * l + g
                            pe.wait_ge(sm["t_updated"], at(n + 1, i, 2 * nl - 2))
                            for h in range(4 * g, 4 * g + 4):
                                m = nc.tensor.transpose(ps[:, 2 * g, (h % 4) * P:(h % 4 + 1) * P], Tm[:, h, :], ident[:, :])
                            m.then_inc(sm["t_turned"], 1)
                pe.wait_ge(sm["gv_ready"], at(1, i, 1))
                pe.wait_ge(sm["inverse_ready"], at(2, i, 2))
                for c in range(2):
                    r = slice(c * CH, (c + 1) * CH)
                    pe.wait_ge(sm["state_ready"], at(c + 1, i, 2))
                    for p in range(HP):
                        m = mm(ps[r, 4, p * P:(p + 1) * P], KR[:, p, 0, r], St[:, p, :], start=True, stop=True)
                    m.then_inc(sm["g_done"], 1)
                    for p in range(HP):
                        mm(ps[:, 5, p * P + c * CH:p * P + (c + 1) * CH], St[:, p, :], KR[:, p, 1, r],
                           start=(c == 0 and p == 0), stop=False, skip_group_check=True)
                    pe.wait_ge(sm["g_ready"], at(c + 1, i, 2))
                    mm(ps[:, 7, 0:P], ktn[r, 0:P], Vt[r, 0:P], start=True, stop=False)
                    for h in range(H):
                        m = mm(ps[r, 6, h * N:(h + 1) * N], Rm[r, h, r], Gs[r, h * N:(h + 1) * N], start=True, stop=True)
                    m.then_inc(sm["u_done"], 1)
                    pe.wait_ge(sm["u_ready"], at(c + 1, i, 2))
                    for p in range(HP):
                        q = slice(p * P, (p + 1) * P)
                        if p:
                            mm(ps[:, 7, q], ktn[r, q], Vt[r, q], start=True, stop=False)
                        m = mm(ps[:, 7, q], btn[r, q], Un[r, q], start=False, stop=True)
                    m.then_inc(sm["x_done"], 1)
                for h in range(H):
                    p, e = h // 2, h % 2
                    o = ps[64 * e:64 * e + 64, 5, p * P:(p + 1) * P]
                    v = slice(h * N, (h + 1) * N)
                    mm(o, Vt[:, v], KA[:, p, e, 1, :], start=False, stop=False, skip_group_check=True)
                    m = mm(o, Un[:, v], LA[:, p, e, 1, :], start=False, stop=h == H - 1, skip_group_check=True)
                m.then_inc(sm["y_done"], 1)

            pe.wait_ge(sm["y_ready"], NB + 1)
            for p in range(HP):
                mm(ps[:, p, :], ones64[:, :], vy[:, p, :], start=True, stop=True).then_inc(sm["mean_done"], 1)
            for p in range(HP):
                pe.wait_ge(sm["centred_sq"], p + 1)
                mm(ps[:, 4 + p, :], ones64[:, :], hsq[:, p % 2, :], start=True, stop=True).then_inc(sm["var_done"], 1)
            pe.wait_ge(sm["gn_sd"], HP)

            def attention(b):
                def scores(n):
                    e, t = n // TT, n % TT
                    mm(ps[:, 2 + n % 4, 0:(t + 1) * P], qs[:, t * P:(t + 1) * P], (ks0, ks1)[e][:, 0:(t + 1) * P],
                       start=True, stop=True).then_inc(sm["s_done"], 1)

                def turn(i, n):
                    t = n % TT
                    pe.wait_ge(sm["p_ready"], at(32 * b + n + 1, i, 8))
                    for j in range(t + 1):
                        m = nc.tensor.transpose(ps[:, 6 + n % 2, j * P:(j + 1) * P], Pm[:, n % 2, j * P:(j + 1) * P], ident[:, :])
                    m.then_inc(sm["p_turned"], 1)

                def values(i, n):
                    e, t = n // TT, n % TT
                    if t == 0:
                        pe.wait_ge(sm["o_ready"], at(8 * b + e + 1, i, 2))
                    pe.wait_ge(sm["pt_ready"], at(32 * b + n + 1, i, 8))
                    for j in range(t + 1):
                        m = mm(ps[:, e, t * N:(t + 1) * N], PT[:, n % 2, j * P:(j + 1) * P],
                               Vn[:, j, bass.ds(i * P + e * N, N)], start=j == 0, stop=j == t)
                    m.then_inc(sm["pv_done"], 1)

                pe.wait_ge(sm["tile_evacuated"], T_OUT1 if b == 0 else T_OUT2)
                with pe.Fori(0, HP) as i:
                    pe.wait_ge(sm["pair_staged"], at(4 * b + 1, i, 1))
                    scores(0)
                    scores(1)
                    scores(2)
                    for n in range(8):
                        turn(i, n)
                        if n + 3 < 8:
                            scores(n + 3)
                        if n >= 1:
                            values(i, n - 1)
                    values(i, 7)
                for c in range(HP):
                    pe.wait_ge(sm["o_scaled"], TT * (b + 1))
                    if c >= 2:
                        pe.wait_ge(sm["mix_f32"], HP * b + c - 1)
                    for t in range(TT):
                        m = nc.tensor.transpose(ps[:, 4 + c % 2, t * P:(t + 1) * P], On[:, t, c * P:(c + 1) * P], ident[:, :])
                    m.then_inc(sm["o_turned"], 1)

            attention(0)
            for c in range(4):
                product(G_OUT1 + c, T_OUT1 + 2 * c, [(T_OUT1 + 2 * c + j) % 4 for j in range(2)], 0, h_hi, h_lo,
                        lower=H_OUT1 if c == 0 else None)
                if c in (1, 2):
                    turn_x(1, range(4 * (c - 1), 4 * c))
            square_total(0)
            square_sums(1)
            ffn(G_FFN1, T_FFN1, H_FFN1)
            square_total(1)
            square_sums(2)
            for c in range(2):
                product(G_U2 + c, T_U2 + 2 * c, [(T_U2 + 2 * c + j) % 4 for j in range(2)], 0, h_hi, h_lo,
                        lower=H_MIX2 if c == 0 else None)
            product_loop(G_QK2, T_QK2, 2)
            product_natural(G_V2, T_V2)
            pe.wait_ge(sm["wpool_loaded"], 16)
            for g in range(4):
                pe.wait_ge(sm["window_ready"], g + 1)
                if g >= 2:
                    pe.wait_ge(sm["pool_scaled"], g - 1)
                mm(ps[:, 6 + g % 2, :], wpool[:, g, :], uT[:, g, :], start=True, stop=True).then_inc(sm["pooled"], 1)
            pe.wait_ge(sm["pool_scaled"], 4)
            attention(1)
            product_loop(G_OUT2, T_OUT2, 2, lower=H_OUT2)
            square_total(2)
            ffn(G_FFN2, T_FFN2, H_FFN2)
            square_total(3)
            for k in range(KT):
                pe.wait_ge(sm["out_f32"], k + 1)
                if k >= 2:
                    pe.wait_ge(sm["out_ready"], k - 1)
                for t in range(TT):
                    m = nc.tensor.transpose(ps[:, 4 + k % 2, t * P:(t + 1) * P], tmp[:, k % 4, t * P:(t + 1) * P], ident[:, :])
                m.then_inc(sm["out_turned"], 1)

        @blk.scalar
        def _(act):
            af = nc.scalar.activation

            def split(g, i=None, per=0, n=GW):
                act.wait_ge(w_in[g % 2], at(16 * (g // 2 + 1), i, 8 * per))
                if not (i is None and g < 2):
                    act.wait_ge(sm["mm_done"], at(2 * (g - 1), i, 2 * per))
                af(w_hi[:, g % 2, :, 0:n], w_raw[:, g % 2, :, 0:n], ACT.Copy).then_inc(sm["w_hi_ready"], 1)

            def evacuate(g, j, tile, dst, i=None, per=0, func=ACT.Copy):
                act.wait_ge(sm["mm_done"], at(2 * g + j + 1, i, 2 * per))
                af(dst, ps[:, tile % 4, :], func).then_inc(sm["tile_evacuated"], 1)

            def turned_x(load, tiles=range(KT)):
                for k in tiles:
                    act.wait_ge(sm["x_turned"], 8 * load + k + 1)
                    af(xT[:, k, :], ps[:, 4 + k % 2, :], ACT.Copy).then_inc(sm["x_ready"], 1)

            def squares(n, src, ready, base):
                for k in range(KT):
                    act.wait_ge(sm[ready], base + k + 1)
                    if 8 * n + k >= 2:
                        act.wait_ge(sm["sq_used"], 8 * n + k - 1)
                    af(hsq[:, k % 2, :], src[:, k, :], ACT.Square).then_inc(sm["sq_ready"], 1)
                act.wait_ge(sm["sq_used"], 8 * n + 8)
                root()

            def root():
                af(rstd[:, :], ps[:, 6, :], ACT.Sqrt, bias=eps[:, 0:1], scale=1.0 / D).then_inc(sm["sd_ready"], 1)

            def root_of_total(n):
                act.wait_ge(sm["sum_made"], n + 1)
                root()

            def upper(n):
                for k in range(KT):
                    act.wait_ge(sm["hf_ready"], KT * n + k + 1)
                    af(h_hi[:, k, :], tmp[:, k % 4, :], ACT.Copy).then_inc(sm["hhi_ready"], 1)

            def ffn(g, tile, b):
                for half in range(2):
                    with act.Fori(0, HT // 4) as i:
                        for c in range(2):
                            split(g + c + 1, i, 2)
                            for j in range(2):
                                m = 2 * c + j
                                n = (2 * b + half) * HT + m
                                act.wait_ge(sm["squared"], at(n + 1, i, 4))
                                evacuate(g + c, j, tile + m, tmp[:, m, :], i, 2, ACT.Relu)
                    g, tile = g + HT // 2, tile + HT

                    def down(c0, i, last=False):
                        for c in range(4):
                            if not (last and c == 3):
                                split(g + c0 + c + 1, i, 4)
                            if c % 2:
                                for j in range(2):
                                    m = 2 * (c // 2) + j
                                    evacuate(g + c0 + c, j, tile + c0 + m, tmp[:, m, :], i, 4)

                    if b == 1 and half == 1:
                        down(0, None)
                        down(4, None, last=True)
                    else:
                        with act.Fori(0, 2) as i:
                            down(0, i)
                    g, tile = g + 8, tile + 8

            act.wait_ge(sm["page_turned"], 1)
            af(par[:, 0:PAGE_ROWS], ps[:, 7, 0:PAGE_ROWS], ACT.Copy).then_inc(sm["par_ready"], 1)
            turned_x(0)
            split(G_LORA, n=160)
            act.wait_ge(sm["consts_built"], 1)
            squares(0, xT, "x_ready", X_LOAD1)
            upper(0)
            split(G_RKV)
            for j in range(2):
                act.wait_ge(sm["mm_done"], j + 1)
                act.wait_ge(sm["consts_built"], 2)
                af(zraw[:, j, 1:S + 1], ps[:, j, :], ACT.Copy).then_inc(sm["tile_evacuated"], 1)
            act.wait_ge(sm["shifted"], 2)
            def rkv_tiles(g, tile, i=None):
                for c in range(2):
                    split(g + c + 1, i, 2)
                    for j in range(2):
                        m = 2 * c + j
                        act.wait_ge(sm["shifted"], at(tile + m - 1, i, 4))
                        evacuate(g + c, j, tile + m, zraw[:, m % 2, 1:S + 1], i, 2)

            rkv_tiles(G_RKV, T_RKV)
            af(xwa[0:32, :], xwa[0:32, :], ACT.Tanh)
            af(xag[:, :], xag[:, :], ACT.Sigmoid).then_inc(sm["lora_act"], 1)
            with act.Fori(0, HP) as p:
                act.wait_ge(sm["lora_mm"], at(1, p, 1))
                af(kap[:, p, :], ps[:, 4, :], ACT.Sigmoid, bias=cols("decay_w0", p))
                af(bh[:, p, :], ps[:, 5, :], ACT.Sigmoid, bias=cols("aaa_a0", p))
                af(gT[:, p, :], ps[:, 6, :], ACT.Copy).then_inc(sm["lora_evacuated"], 1)
            with act.Fori(0, 2) as i:
                rkv_tiles(G_RKV + 2, T_RKV + 4, i)

            def qk(g, tile, rwkv=False):
                with act.Fori(0, 2) as i:
                    for c in range(2):
                        split(g + c + 1, i, 2)
                        if rwkv:
                            act.wait_ge(sm["prep_done"], at(c + 1, i, 2))
                            act.wait_ge(sm["prep_pool"], at(c + 1, i, 2))
                            af(tmp[:, 0, :], rk[:, i * 2 + HP + c, :], ACT.Copy, scale=cols("k_k", i * 2 + c))
                            act.drain()
                            af(hsq[:, 0, :], tmp[:, 0, :], ACT.Square).then_inc(sm["kk_sq"], 1)
                            act.wait_ge(sm["cum_ready"], at(c + 1, i, 2))
                            af(eD, tmp[:, 3, :], ACT.Exp, scale=-EXP_MHALF)
                            af(eI, tmp[:, 3, :], ACT.Exp, scale=EXP_MHALF)
                            act.wait_ge(sm["lx_ready"], at(c + 1, i, 2))
                            af(eE, lx, ACT.Exp, scale=-EXP_MHALF).then_inc(sm["decays_ready"], 1)
                            act.wait_ge(sm["kk_ss"], at(c + 1, i, 2))
                            af(nrm, ps[:, 7, :], ACT.Sqrt).then_inc(sm["kk_norm"], 1)
                        for j in range(2):
                            m = 2 * c + j
                            evacuate(g + c, j, tile + m, qkT[:, i * 4 + m, :], i, 2)

            def natural_v(g, tile):
                for c in range(2):
                    split(g + c + 1)
                    for b in range(2):
                        act.wait_ge(sm["mm_done"], 2 * (g + c) + b + 1)
                        af(Vn[:, 2 * b:2 * b + 2, c * GW:(c + 1) * GW],
                           ps[:, (tile + 2 * c + b) % 4, :].rearrange("p (t n) -> p t n", t=2), ACT.Copy)\
                            .then_inc(sm["tile_evacuated"], 1)

            qk(G_QK1, T_QK1, rwkv=True)
            natural_v(G_V1, T_V1)
            nl = len(LEVELS)
            act.wait_ge(sm["prep_done"], HP + 1)
            act.wait_ge(sm["prep_pool"], HP + 1)
            with act.Fori(0, NB) as i:
                af(KR[:, :, 0, :], block(kap[:, :, :], i), ACT.Copy)
                af(KR[:, :, 1, :], block(rk[:, 0:HP, :], i), ACT.Copy).then_inc(sm["block_staged_act"], 1)
                for n, dst in enumerate((Vt, ktn, btn)):
                    act.wait_ge(sm["block_turned"], at(n + 1, i, 3))
                    af(dst, ps[:, n, :], ACT.Copy).then_inc(sm["natural_ready"], 1)
                for g in range(2):
                    act.wait_ge(sm["t0_turned"], at(g + 1, i, 2))
                    af(Tm[:, 4 * g:4 * g + 4, :], ps[:, 2 * g, :].rearrange("p (h t) -> p h t", t=P), ACT.Copy)\
                        .then_inc(sm["t_ready"], 1)
                act.wait_ge(sm["gv_done"], at(1, i, 1))
                af(GV, ps[:, 4, :], ACT.Copy).then_inc(sm["gv_ready"], 1)
                for l in range(nl):
                    for g in range(2):
                        act.wait_ge(sm["q_done"], at(2 * l + g + 1, i, 2 * nl))
                        af(Qm[:, 4 * g:4 * g + 4, :], ps[:, 2 * g, :].rearrange("p (h t) -> p h t", t=P), ACT.Copy)\
                            .then_inc(sm["q_ready"], 1)
                    if l < nl - 1:
                        for g in range(2):
                            act.wait_ge(sm["t_turned"], at(2 * l + g + 1, i, 2 * nl - 2))
                            af(Rm[:, 4 * g:4 * g + 4, :], ps[:, 2 * g, :].rearrange("p (h t) -> p h t", t=P), ACT.Copy)\
                                .then_inc(sm["r_ready"], 1)
                for c in range(2):
                    r = slice(c * CH, (c + 1) * CH)
                    act.wait_ge(sm["u_done"], at(c + 1, i, 2))
                    af(Un[r, :], ps[r, 6, :], ACT.Copy, scale=-1.0).then_inc(sm["u_ready"], 1)
                act.wait_ge(sm["y_done"], at(1, i, 1))
                af(block(vy, i), ps[:, 5, :].rearrange("p (h t) -> p h t", t=P), ACT.Copy).then_inc(sm["y_ready"], 1)
            for p in range(HP):
                af(bonus[:, p, :], bonus[:, p, :], ACT.Identity, bias=cols("gn_b", p))
            for p in range(HP):
                act.wait_ge(sm["centred"], p + 1)
                if p >= 2:
                    act.wait_ge(sm["var_done"], p - 1)
                af(hsq[:, p % 2, :], tmp[:, p, :], ACT.Square).then_inc(sm["centred_sq"], 1)
            for p in range(HP):
                act.wait_ge(sm["var_done"], p + 1)
                af(vy[:, p, :], ps[:, 4 + p, :], ACT.Sqrt, bias=eps[:, 1:2], scale=1.0 / N).then_inc(sm["gn_sd"], 1)

            def attention(b):
                with act.Fori(0, HP) as i:
                    for n in range(9):
                        if n < 8:
                            t = n % TT
                            act.wait_ge(sm["max_ready"], at(32 * b + n + 1, i, 8))
                            af(Pm[:, n % 2, 0:(t + 1) * P], Z[:, n % 2, 0:(t + 1) * P], ACT.Exp, bias=negmax[:, n:n + 1],
                               scale=-1.0, accum_out=rowsum[:, n:n + 1]).then_inc(sm["p_ready"], 1)
                        if n == 0:
                            continue
                        n, t = n - 1, (n - 1) % TT
                        act.wait_ge(sm["p_turned"], at(32 * b + n + 1, i, 8))
                        af(PT[:, n % 2, 0:(t + 1) * P], ps[:, 6 + n % 2, 0:(t + 1) * P], ACT.Copy).then_inc(sm["pt_ready"], 1)
                if b == 0:
                    act.wait_ge(sm["o_ready"], 8 + 2)
                    for t in range(TT):
                        if t >= 1:
                            act.drain()
                        af(ks1[:, :], On[:, t, :], ACT.Square, accum_out=osq[:, t:t + 1]).then_inc(sm["o_sq"], 1)
                    act.drain()
                    af(osq[:, :], osq[:, :], ACT.Sqrt, bias=eps[:, 0:1], scale=1.0 / 512).then_inc(sm["o_sd"], 1)
                    act.wait_ge(sm["gn_done"], HP)
                for c in range(HP):
                    act.wait_ge(sm["o_turned"], HP * b + c + 1)
                    if b == 0:
                        af(tmp[:, c, :], ps[:, 4 + c % 2, :], ACT.Copy, scale=cols("attn_out_gain", c)).then_inc(sm["mix_f32"], 1)
                    else:
                        af(tmp[:, c, :], ps[:, 4 + c % 2, :], ACT.Copy).then_inc(sm["mix_f32"], 1)
                    act.drain()
                    af(h_hi[:, c, :], tmp[:, c, :], ACT.Copy).then_inc(sm["hhi_ready"], 1)

            def second_half(src):
                for p in range(HP):
                    af(h_hi[:, HP + p, :], src[:, p, :], ACT.Copy).then_inc(sm["hhi_ready"], 1)

            def out_product(g, tile):
                with act.Fori(0, 2) as i:
                    for c in range(2):
                        split(g + c + 1, i, 2)
                        for j in range(2):
                            m = 2 * c + j
                            act.wait_ge(sm["x_ready"], at(X_MIX2 + m - 3, i, 4))
                            evacuate(g + c, j, tile + m, tmp[:, m, :], i, 2)

            attention(0)
            second_half(vy)
            for c in range(4):
                split(G_OUT1 + c + 1)
                for j in range(2):
                    evacuate(G_OUT1 + c, j, T_OUT1 + 2 * c + j, yT[:, 2 * c + j, :])
                if c in (1, 2):
                    turned_x(1, range(4 * (c - 1), 4 * c))
            root_of_total(0)
            squares(1, xT, "x_ready", X_MIX1)
            upper(1)
            ffn(G_FFN1, T_FFN1, 0)
            root_of_total(1)
            squares(2, xT, "x_ready", X_FFN1)
            upper(2)
            for c in range(2):
                split(G_U2 + c + 1)
                for j in range(2):
                    evacuate(G_U2 + c, j, T_U2 + 2 * c + j, uT[:, 2 * c + j, :])
            qk(G_QK2, T_QK2)
            natural_v(G_V2, T_V2)
            for g in range(4):
                act.wait_ge(sm["pooled"], g + 1)
                af(uT[:, g, :], ps[:, 6 + g % 2, :], ACT.Copy, scale=cols("pool_scale_2", g)).then_inc(sm["pool_scaled"], 1)
            attention(1)
            second_half(uT)
            out_product(G_OUT2, T_OUT2)
            root_of_total(2)
            upper(3)
            ffn(G_FFN2, T_FFN2, 1)
            root_of_total(3)
            for k in range(KT):
                act.wait_ge(sm["out_turned"], k + 1)
                af(xn[:, :, k * P:(k + 1) * P], ps[:, 4 + k % 2, :].rearrange("p (t n) -> p t n", t=TT), ACT.Copy)\
                    .then_inc(sm["out_ready"], 1)

        @blk.vector
        def _(dve):
            v = nc.vector

            def split(g, i=None, per=0, n=GW):
                dve.wait_ge(sm["w_hi_ready"], at(g + 1, i, per))
                v.tensor_tensor(w_lo[:, g % 2, :, 0:n], w_raw[:, g % 2, :, 0:n], w_hi[:, g % 2, :, 0:n].bitcast(F32),
                                ALU.subtract).then_inc(sm["w_lo_ready"], 1)

            def inverse_root(n):
                dve.wait_ge(sm["sd_ready"], n + 1)
                v.reciprocal(rstd[:, :], rstd[:, :]).then_inc(sm["rstd_ready"], 1)
                dve.drain()

            def lower(h, k, src):
                dve.wait_ge(sm["hhi_ready"], h + k + 1)
                v.tensor_tensor(h_lo[:, k, :], src, h_hi[:, k, :].bitcast(F32), ALU.subtract).then_inc(sm["hlo_ready"], 1)

            def normed(h, gain):
                for k in range(KT + 1):
                    if k < KT:
                        v.scalar_tensor_tensor(out=tmp[:, k % 4, :], in0=xT[:, k, :], scalar=cols(gain, k), in1=rstd[:, :],
                                               op0=ALU.mult, op1=ALU.mult).then_inc(sm["hf_ready"], 1)
                    if k >= 1:
                        lower(h, k - 1, tmp[:, (k - 1) % 4, :])

            def add_normed(gain):
                for k in range(KT):
                    v.scalar_tensor_tensor(out=tmp[:, k % 4, :], in0=yT[:, k, :], scalar=cols(gain, k), in1=rstd[:, :],
                                           op0=ALU.mult, op1=ALU.mult)
                    dve.drain()
                    v.tensor_tensor(xT[:, k, :], xT[:, k, :], tmp[:, k % 4, :], ALU.add).then_inc(sm["x_ready"], 1)
                dve.drain()

            def ffn(g, tile, b):
                for half in range(2):
                    with dve.Fori(0, HT // 4) as i:
                        for c in range(2):
                            split(g + c + 1, i, 2)
                            for j in range(2):
                                m = 2 * c + j
                                dve.wait_ge(sm["tile_evacuated"], at(tile + m + 1, i, 4))
                                v.tensor_tensor(a_hi[:, i * 4 + m, :], tmp[:, m, :], tmp[:, m, :], ALU.mult)
                            dve.drain()
                            for j in range(2):
                                m = 2 * c + j
                                dve.wait_ge(sm["square_f32"], at((2 * b + half) * HT + m + 1, i, 4))
                                v.tensor_tensor(a_lo[:, i * 4 + m, :], hsq[:, m % 2, :], a_hi[:, i * 4 + m, :].bitcast(F32),
                                                ALU.subtract).then_inc(sm["squared"], 1)
                    g, tile = g + HT // 2, tile + HT

                    def down(c0, i, last=False):
                        for c in range(4):
                            if not (last and c == 3):
                                split(g + c0 + c + 1, i, 4)
                            if c % 2:
                                for j in range(2):
                                    m = 2 * (c // 2) + j
                                    dve.wait_ge(sm["tile_evacuated"], at(tile + c0 + m + 1, i, 4))
                                    k = c0 + m if i is None else i * 4 + m
                                    acc = (yT if b == 0 else xT)[:, k, :]
                                    done = "y_added" if b == 0 else "x_ready"
                                    if b == 0 and half == 0:
                                        v.tensor_copy(acc, tmp[:, m, :]).then_inc(sm[done], 1)
                                    else:
                                        v.tensor_tensor(acc, acc, tmp[:, m, :], ALU.add).then_inc(sm[done], 1)

                    if b == 1 and half == 1:
                        down(0, None)
                        down(4, None, last=True)
                    else:
                        with dve.Fori(0, 2) as i:
                            down(0, i)
                    g, tile = g + 8, tile + 8

            dve.wait_ge(sm["consts_built"], 2)
            di = xwa[:, :].bitcast(I32)
            m4, m16, m128 = tmp[:, 0, :], tmp[:, 1, :], tmp[:, 2, :]
            v.tensor_scalar(tmp[:, 3, :].bitcast(I32), di, 3, None, ALU.bitwise_and)
            v.tensor_scalar(tmp[:, 2, :].bitcast(I32), di, 15, None, ALU.bitwise_and)
            dve.drain()
            v.tensor_scalar(m4, tmp[:, 3, :].bitcast(I32), 0.0, None, ALU.is_equal)
            v.tensor_scalar(m16, tmp[:, 2, :].bitcast(I32), 0.0, None, ALU.is_equal)
            dve.drain()
            v.tensor_scalar(m128, delta[:, :], 128.0, None, ALU.is_le)
            dve.drain()
            v.tensor_tensor(m4, m4, m16, ALU.add)
            dve.drain()
            v.tensor_tensor(m4, m4, m128, ALU.add)
            v.tensor_scalar(tmp[:, 3, :], delta[:, :], 0.0, None, ALU.is_ge)
            dve.drain()
            v.tensor_tensor(m4, m4, tmp[:, 3, :], ALU.mult)
            dve.drain()
            v.tensor_scalar(lncount[:, :], m4, 1.0, BIG, ALU.is_lt, ALU.mult)
            v.tensor_scalar(m16, m4, 2.0, -LN2, ALU.is_ge, ALU.mult)
            v.tensor_scalar(m128, m4, 3.0, -LN32, ALU.is_ge, ALU.mult)
            dve.drain()
            v.tensor_tensor(lncount[:, :], lncount[:, :], m16, ALU.add)
            v.tensor_scalar(tmp[:, 3, :], delta[:, :], 0.0, BIG, ALU.is_lt, ALU.mult)
            dve.drain()
            v.tensor_tensor(lncount[:, :], lncount[:, :], m128, ALU.add)
            v.tensor_tensor(delta[:, :], delta[:, :], tmp[:, 3, :], ALU.add)
            dve.drain()

            split(G_LORA, n=160)
            inverse_root(N_MIX1)
            dve.wait_ge(sm["par_ready"], 1)
            normed(H_MIX1, "norm_mix_pre")
            split(G_RKV)

            def shift(slot, dst, mu):
                v.tensor_tensor(tmp[:, slot, :], zraw[:, slot, 0:S], zraw[:, slot, 1:S + 1], ALU.subtract)
                dve.drain()
                v.scalar_tensor_tensor(out=dst, in0=tmp[:, slot, :], scalar=mu, in1=zraw[:, slot, 1:S + 1],
                                       op0=ALU.mult, op1=ALU.add).then_inc(sm["shifted"], 1)

            for j, (dst, mu) in enumerate(((xwa, "mu_wa"), (xag, "mu_ag"))):
                dve.wait_ge(sm["tile_evacuated"], j + 1)
                shift(j, dst[:, :], cols(mu))
            with dve.Fori(0, 3) as i:
                for c in range(2):
                    split(G_RKV + c + 1, i, 2)
                    for j in range(2):
                        m = 2 * c + j
                        dve.wait_ge(sm["tile_evacuated"], at(T_RKV + m + 1, i, 4))
                        shift(j, rkv[:, i * 4 + m, :], cols("mu", i * 4 + m))

            dve.drain()
            dve.nop().then_inc(sm["prep_done"], 1)
            with dve.Fori(0, 2) as i:
                for c in range(2):
                    p = i * 2 + c
                    k_, r_, v_ = rk[:, p + HP, :], rk[:, p, :], vy[:, p, :]
                    split(G_QK1 + c + 1, i, 2)
                    dve.wait_ge(sm["prep_pool"], at(c + 1, i, 2))
                    v.tensor_tensor_scan(tmp[:, 3, :], starts[:, :], kap[:, p, :], 0.0, ALU.mult, ALU.add)\
                        .then_inc(sm["cum_ready"], 1)
                    v.tensor_scalar(tmp[:, 1, :], bh[:, p, :], -1.0, cols("k_a", p), ALU.add, ALU.mult)
                    dve.drain()
                    dve.wait_ge(sm["kk_sq"], at(c + 1, i, 2))
                    v.scalar_tensor_tensor(out=k_, in0=tmp[:, 1, :], scalar=1.0, in1=k_, op0=ALU.add, op1=ALU.mult)
                    dve.drain()
                    v.scalar_tensor_tensor(out=tmp[:, 1, :], in0=r_, scalar=cols("r_k", p), in1=k_, op0=ALU.mult, op1=ALU.mult)\
                        .then_inc(sm["bonus_in"], 1)
                    dve.wait_ge(sm["decays_ready"], at(c + 1, i, 2))
                    v.tensor_tensor(k_, k_, eI, ALU.mult)
                    v.tensor_copy(dC[:, p, :], eD[:, CH - 1:S:CH])
                    dve.wait_ge(sm["kk_norm"], at(c + 1, i, 2))
                    v.tensor_scalar(nrm, nrm, 1e-12, None, ALU.max)
                    dve.drain()
                    v.reciprocal(nrm, nrm)
                    dve.drain()
                    v.tensor_tensor(tmp[:, 2, :], tmp[:, 0, :], nrm, ALU.mult).then_inc(sm["kk_ready"], 1)
                    dve.wait_ge(sm["bonus_sum"], at(c + 1, i, 2))
                    v.tensor_tensor(bonus[:, p, :], ps[:, 6, :], v_, ALU.mult)
                    dve.drain()
                    v.tensor_tensor(kap[:, p, :], tmp[:, 2, :], eE, ALU.mult).then_inc(sm["prep_done"], 1)
            for c in range(2):
                split(G_V1 + c + 1)
            dve.drain()
            nl = len(LEVELS)
            with dve.Fori(0, NB) as i:
                dve.wait_ge(sm["y_ready"], at(1, i, 1))
                dve.wait_ge(sm["prep_pool"], HP + 1)
                dce = dC[:, :, bass.ds(i * 2, 2)].unsqueeze(3).broadcast_to([P, HP, 2, CH])
                for dst, src in ((ktb, rk[:, HP:2 * HP, :]), (btb, bh[:, :, :])):
                    v.tensor_tensor(dst[:, :, :].rearrange("p h (c t) -> p h c t", t=CH),
                                    block(src, i).rearrange("p h (c t) -> p h c t", t=CH), dce, ALU.mult)\
                        .then_inc(sm["block_staged_dve"], 1)
                for kind, dst in enumerate((LA, KA)):
                    for b in range(4):
                        e, g = b % 2, b // 2
                        dve.wait_ge(sm["gram_done"], at(4 * kind + b + 1, i, 8))
                        v.tensor_tensor(dst[:, 2 * g:2 * g + 2, e, :, :].rearrange("p h a t -> p h (a t)"),
                                        ps[:, 4 + b, :].rearrange("p (h t) -> p h t", h=2),
                                        tri[:, :, :].rearrange("p a t -> p (a t)").unsqueeze(1).broadcast_to([P, 2, 2 * P]),
                                        ALU.mult).then_inc(sm["gram_masked"], 1)
                for l in range(nl):
                    for g in range(2):
                        hs = slice(4 * g, 4 * g + 4)
                        dt = ps[:, 2 * g + 1, :].rearrange("p (h t) -> p h t", t=P)
                        dve.wait_ge(sm["dt_done"], at(2 * l + g + 1, i, 2 * nl))
                        if l < nl - 1:
                            v.tensor_tensor(Tm[:, hs, :], Tm[:, hs, :], dt, ALU.subtract).then_inc(sm["t_updated"], 1)
                        else:
                            v.tensor_tensor(Rm[:, hs, :], Rm[:, hs, :], dt, ALU.subtract).then_inc(sm["inverse_ready"], 1)
                for c in range(2):
                    r = slice(c * CH, (c + 1) * CH)
                    if c == 1:
                        dve.drain()
                    v.tensor_tensor(Sd[:, :, :], St[:, :, :], dC[:, :, bass.ds(i * 2 + c, 1)].broadcast_to([P, HP, P]), ALU.mult)
                    dve.wait_ge(sm["g_done"], at(c + 1, i, 2))
                    v.tensor_tensor(Gs[r, :], ps[r, 4, :], GV[r, :], ALU.add).then_inc(sm["g_ready"], 1)
                    xs = ps[:, 7, :].rearrange("p (h n) -> p h n", n=P)
                    dve.wait_ge(sm["x_done"], at(c + 1, i, 2))
                    for e in range(2):
                        q = slice(64 * e, 64 * e + 64)
                        m = v.tensor_tensor(St[q, :, q], Sd[q, :, q], xs[q, :, q], ALU.add)
                    m.then_inc(sm["state_ready"], 1)
            dve.drain()
            for p in range(HP):
                dve.wait_ge(sm["mean_done"], p + 1)
                v.scalar_tensor_tensor(out=tmp[:, p, :], in0=ps[:, p, :], scalar=-1.0 / N, in1=vy[:, p, :], op0=ALU.mult,
                                       op1=ALU.add).then_inc(sm["centred"], 1)
            dve.wait_ge(sm["gn_sd"], HP)
            dve.drain()

            def attention(b):
                bias = lncount if b == 0 else delta

                def output(i, e):
                    dve.wait_ge(sm["pv_done"], at(32 * b + 4 * e + 4, i, 8))
                    v.reciprocal(rinv[:, 4 * e:4 * e + 4], rowsum[:, 4 * e:4 * e + 4])
                    dve.drain()
                    v.tensor_tensor(On[:, :, bass.ds(i * P + e * N, N)], ps[:, e, 0:TT * N].rearrange("p (t n) -> p t n", n=N),
                                    rinv[:, 4 * e:4 * e + 4].unsqueeze(2).broadcast_to([P, TT, N]), ALU.mult)\
                        .then_inc(sm["o_ready"], 1)

                with dve.Fori(0, HP) as i:
                    for n in range(8):
                        e, t = n // TT, n % TT
                        w = (t + 1) * P
                        if n >= 2:
                            dve.wait_ge(sm["p_ready"], at(32 * b + n - 1, i, 8))
                        dve.wait_ge(sm["s_done"], at(32 * b + n + 1, i, 8))
                        v.scalar_tensor_tensor(out=Z[:, n % 2, 0:w], in0=bias[:, (TT - 1 - t) * P:S], scalar=slopes[:, b, i, e:e + 1],
                                               in1=ps[:, 2 + n % 4, 0:w], op0=ALU.mult, op1=ALU.subtract).then_inc(sm["z_ready"], 1)
                        dve.drain()
                        v.tensor_reduce(negmax[:, n:n + 1], Z[:, n % 2, 0:w], AX, ALU.min).then_inc(sm["max_ready"], 1)
                        if b == 0:
                            part = slice(n * S // 8, (n + 1) * S // 8)
                            v.reciprocal(vy[:, i, part], vy[:, i, part])
                        if b == 0 and n == 7:
                            dve.drain()
                            v.scalar_tensor_tensor(out=tmp[:, i, :], in0=tmp[:, i, :], scalar=cols("gn_w", i), in1=vy[:, i, :],
                                                   op0=ALU.mult, op1=ALU.mult).then_inc(sm["gn_scaled"], 1)
                    for e in range(2):
                        output(i, e)
                dve.drain()
                if b == 0:
                    dve.wait_ge(sm["o_sd"], 1)
                    v.reciprocal(osq[:, :], osq[:, :])
                    dve.drain()
                for t in range(TT):
                    if b == 0:
                        v.tensor_scalar(On[:, t, :], On[:, t, :], osq[:, t:t + 1], None, ALU.mult).then_inc(sm["o_scaled"], 1)
                    else:
                        dve.nop().then_inc(sm["o_scaled"], 1)
                for c in range(HP):
                    lower(H_OUT1 if b == 0 else H_OUT2, c, tmp[:, c, :])

            def out_product(g, tile, b):
                with dve.Fori(0, 2) as i:
                    for c in range(2):
                        split(g + c + 1, i, 2)
                        if b == 1:
                            for j in range(2):
                                m = 2 * c + j
                                dve.wait_ge(sm["tile_evacuated"], at(tile + m + 1, i, 4))
                                v.tensor_tensor(xT[:, i * 4 + m, :], xT[:, i * 4 + m, :], tmp[:, m, :], ALU.add)\
                                    .then_inc(sm["x_ready"], 1)

            attention(0)
            for p in range(HP):
                lower(H_OUT1, HP + p, vy[:, p, :])
            out_product(G_OUT1, T_OUT1, 0)
            inverse_root(N_POST1)
            dve.wait_ge(sm["x_ready"], X_LOAD2 + 8)
            add_normed("norm_mix_post")
            inverse_root(N_FFN1)
            normed(H_FFN1, "norm_ffn_pre")
            ffn(G_FFN1, T_FFN1, 0)
            inverse_root(N_FPOST1)
            add_normed("norm_ffn_post")
            inverse_root(N_MIX2)
            normed(H_MIX2, "norm_mix_2")
            for c in range(2):
                split(G_U2 + c + 1)
            dve.wait_ge(sm["consts_built"], 3)
            v.reciprocal(rcnt[:, :, :], rcnt[:, :, :])
            v.memset(upad[:, :, 0:16], 0.0)
            for g in range(4):
                split(G_QK2 + g + 1)
                dve.wait_ge(sm["tile_evacuated"], T_U2 + g + 1)
                v.tensor_copy(upad[:, 0, 16:16 + S], uT[:, g, :])
                dve.drain()
                for s in range(g + 1):
                    src, dst = upad[:, s % 2, :], upad[:, (s + 1) % 2, :]
                    v.tensor_tensor(dst[:, 16:16 + S], src[:, 16:16 + S], src[:, 16 - 2 ** s:16 - 2 ** s + S], ALU.add)
                    dve.drain()
                v.tensor_tensor(upad[:, (g + 1) % 2, 16:16 + S], upad[:, (g + 1) % 2, 16:16 + S], rcnt[:, g, :], ALU.mult)
                dve.drain()
                v.tensor_tensor(uT[:, g, :], upad[:, (g + 1) % 2, 16:16 + S], uT[:, g, :], ALU.subtract)\
                    .then_inc(sm["window_ready"], 1)
                dve.drain()
            for c in range(2):
                split(G_V2 + c + 1)
            attention(1)
            for p in range(HP):
                lower(H_OUT2, HP + p, uT[:, p, :])
            out_product(G_OUT2, T_OUT2, 1)
            dve.drain()
            inverse_root(N_FFN2)
            normed(H_FFN2, "norm_mlp_2")
            ffn(G_FFN2, T_FFN2, 1)
            dve.drain()
            inverse_root(N_FINAL)
            for k in range(KT):
                if k >= 4:
                    dve.wait_ge(sm["out_turned"], k - 3)
                v.scalar_tensor_tensor(out=tmp[:, k % 4, :], in0=xT[:, k, :], scalar=cols("norm_final_2", k), in1=rstd[:, :],
                                       op0=ALU.mult, op1=ALU.mult).then_inc(sm["out_f32"], 1)

        @blk.gpsimd
        def _(pool):
            g_ = nc.gpsimd

            def block_diagonal(x, size):
                view = x.rearrange("p (b t) -> p b t", t=size)
                g_.affine_select(out=view, in_=view, compare_op=ALU.is_ge, fill=0.0, base=0,
                                 pattern=[[-size, P // size], [0, size]], channel_multiplier=1)
                pool.drain()
                g_.affine_select(out=view, in_=view, compare_op=ALU.is_ge, fill=0.0, base=size - 1,
                                 pattern=[[size, P // size], [0, size]], channel_multiplier=-1)
                pool.drain()

            g_.memset(ident[:, :], 0.0)
            g_.memset(ones[:, :], 1.0)
            g_.memset(ones64[:, :], 1.0)
            g_.memset(eps[:, 0:1], RMS_EPS)
            g_.memset(eps[:, 1:2], GN_EPS)
            g_.memset(eps[:, 2:3], N ** -0.5)
            pool.drain()
            g_.affine_select(out=ident[:, :], in_=ident[:, :], compare_op=ALU.not_equal, fill=1.0, base=0,
                             pattern=[[-1, P]], channel_multiplier=1)
            block_diagonal(ones64[:, :], N)
            g_.memset(slopes[:, 0, :, :], 1.0).then_inc(sm["consts_built"], 1)
            g_.memset(zraw[:, :, 0:1], 0.0)
            g_.memset(lora_up[:, :, :], 0.0)
            g_.iota(xwa[:, :].bitcast(I32), pattern=[[-1, S]], base=3 * P, channel_multiplier=1)
            pool.drain()
            g_.tensor_copy(delta[:, :], xwa[:, :].bitcast(I32))
            pool.drain()
            for h in range(H):
                g_.memset(slopes[:, 1, h // 2, h % 2:h % 2 + 1], float(2.0 ** (-8.0 * (h + 1) / H)))
            g_.memset(starts[:, :], 1.0)
            pool.drain()
            g_.memset(starts[:, 0:S:CH], 0.0).then_inc(sm["consts_built"], 1)
            g_.memset(lmask[:, :, :], 1.0)
            g_.memset(tri[:, :, :], 1.0)
            pool.drain()
            for l in range(1 + len(LEVELS)):
                block_diagonal(lmask[:, l, :], 2 ** (l + 1))
            for m in range(2):
                block_diagonal(tri[:, m, :], CH)
            g_.affine_select(out=tri[:, 0, :], in_=tri[:, 0, :], compare_op=ALU.is_gt, fill=0.0, base=0, pattern=[[1, P]],
                             channel_multiplier=-1)
            g_.affine_select(out=tri[:, 1, :], in_=tri[:, 1, :], compare_op=ALU.is_ge, fill=0.0, base=0, pattern=[[1, P]],
                             channel_multiplier=-1)
            pool.drain()
            for l in range(len(LEVELS), 0, -1):
                g_.tensor_tensor(lmask[:, l, :], lmask[:, l, :], lmask[:, l - 1, :], ALU.subtract)
                pool.drain()
            g_.tensor_tensor(lmask[:, 0, :], lmask[:, 0, :], ident[:, :], ALU.subtract)
            pool.drain()
            pool.nop().then_inc(sm["y_ready"], 1)
            pool.nop().then_inc(sm["o_ready"], 2)
            pool.nop().then_inc(sm["prep_pool"], 1)

            for p in range(HP):
                pool.wait_ge(sm["cum_ready"], p + 1)
                g_.tensor_tensor(lx, tmp[:, 3, :], kap[:, p, :], ALU.subtract).then_inc(sm["lx_ready"], 1)
                pool.wait_ge(sm["decays_ready"], p + 1)
                pool.wait_ge(sm["bonus_in"], p + 1)
                g_.tensor_tensor(rk[:, p, :], rk[:, p, :], eD, ALU.mult)
                g_.tensor_tensor(bh[:, p, :], bh[:, p, :], eI, ALU.mult)
                pool.drain()
                pool.wait_ge(sm["kk_ready"], p + 1)
                g_.tensor_tensor(bh[:, p, :], bh[:, p, :], tmp[:, 2, :], ALU.mult).then_inc(sm["prep_pool"], 1)
            pool.wait_ge(sm["prep_done"], HP + 1)
            pool.wait_ge(sm["prep_pool"], HP + 1)
            g_.memset(St[:, :, :], 0.0).then_inc(sm["state_ready"], 1)
            nl = len(LEVELS)
            Lv = LA[:, :, :, :, :].rearrange("p h e a t -> p (h e) a t")
            with pool.Fori(0, NB) as i:
                pool.wait_ge(sm["y_ready"], at(1, i, 1))
                g_.tensor_copy(vb[:, :, :], block(vy, i)).then_inc(sm["block_staged_pool"], 1)
                g_.tensor_copy(bhb[:, :, :], block(bh[:, :, :], i)).then_inc(sm["block_staged_pool"], 1)
                g_.tensor_copy(khb[:, :, :], block(rk[:, HP:2 * HP, :], i)).then_inc(sm["block_staged_pool"], 1)
                for g in range(2):
                    hs = slice(4 * g, 4 * g + 4)
                    pool.wait_ge(sm["gram_masked"], at(2 * g + 2, i, 8))
                    g_.tensor_tensor(Mt[:, hs, :], Lv[:, hs, 0, :], four(lmask[:, 0, :]), ALU.mult)
                    pool.drain()
                    g_.tensor_tensor(Rm[:, hs, :], four(ident[:, :]), Mt[:, hs, :], ALU.subtract).then_inc(sm["r0_ready"], 1)
                for l in range(nl):
                    for g in range(2):
                        hs = slice(4 * g, 4 * g + 4)
                        if l == 0:
                            pool.drain()
                        else:
                            pool.wait_ge(sm["q_done"], at(2 * (l - 1) + g + 1, i, 2 * nl))
                        g_.tensor_tensor(Mt[:, hs, :], Lv[:, hs, 0, :], four(lmask[:, l + 1, :]), ALU.mult)\
                            .then_inc(sm["m_ready"], 1)

            def gate(p):
                pool.wait_ge(sm["gn_scaled"], p + 1)
                g_.tensor_tensor(vy[:, p, :], tmp[:, p, :], bonus[:, p, :], ALU.add)
                pool.drain()
                g_.tensor_tensor(vy[:, p, :], vy[:, p, :], gT[:, p, :], ALU.mult).then_inc(sm["gn_done"], 1)
                pool.drain()

            def clear_keys():
                g_.memset(ks0[64:P, :], 0.0)
                g_.memset(ks1[0:64, :], 0.0)
                pool.drain()

            def stage_pair(i):
                g_.tensor_copy(ks0[0:64, :], qkT[0:64, i + HP, :])
                g_.tensor_copy(ks1[64:P, :], qkT[64:P, i + HP, :])
                pool.drain()
                g_.tensor_tensor(qs[:, :], qkT[:, i, :], eps[:, 2:3].broadcast_to([P, S]), ALU.mult)\
                    .then_inc(sm["pair_staged"], 1)
                pool.drain()

            def squares_f32(tile, b):
                for half in range(2):
                    with pool.Fori(0, HT // 4) as i:
                        for m in range(4):
                            n = (2 * b + half) * HT + m
                            pool.wait_ge(sm["tile_evacuated"], at(tile + m + 1, i, 4))
                            pool.wait_ge(sm["squared"], at(n + 3, i, 4))
                            g_.tensor_tensor(hsq[:, m % 2, :], tmp[:, m, :], tmp[:, m, :], ALU.mult)\
                                .then_inc(sm["square_f32"], 1)
                    tile += HT + 8

            def add_squares(src, ready, base):
                for k in range(KT):
                    pool.wait_ge(sm[ready], base + k + 1)
                    m = g_.tensor_tensor(hsq[:, min(k, 1), :], src[:, k, :], src[:, k, :], ALU.mult)
                    pool.drain()
                    if k:
                        m = g_.tensor_tensor(hsq[:, 0, :], hsq[:, 0, :], hsq[:, 1, :], ALU.add)
                        if k < KT - 1:
                            pool.drain()
                m.then_inc(sm["tiles_summed"], 1)

            pool.wait_ge(sm["y_ready"], NB + 1)
            clear_keys()
            for p in range(HP):
                if p:
                    pool.wait_ge(sm["s_done"], 8 * p)
                stage_pair(p)
                if p:
                    gate(p - 1)
            gate(HP - 1)
            add_squares(yT, "tile_evacuated", T_OUT1)
            pool.nop().then_inc(sm["squared"], 4)
            squares_f32(T_FFN1, 0)
            add_squares(yT, "y_added", HT // 2)
            pool.wait_ge(sm["tile_evacuated"], T_U2 + 1)
            pool.dma_start(wpool[:, :, :], a["w_pool_2"][0].rearrange("g c d -> c g d")).then_inc(sm["wpool_loaded"], 16)
            g_.iota(upad[:, 0, 0:S].bitcast(I32), pattern=[[1, S]], base=1, channel_multiplier=0)
            pool.drain()
            for g in range(4):
                g_.tensor_copy(rcnt[:, g, :], upad[:, 0, 0:S].bitcast(I32))
            pool.drain()
            for g in range(4):
                m = g_.tensor_scalar(rcnt[:, g, :], rcnt[:, g, :], float(2 ** (g + 1)), None, ALU.min)
            m.then_inc(sm["consts_built"], 1)
            pool.wait_ge(sm["tile_evacuated"], T_V2)
            clear_keys()
            with pool.Fori(0, HP) as i:
                stage_pair(i)
                pool.wait_ge(sm["s_done"], at(8 * (HP + 1), i, 8))
            add_squares(xT, "x_ready", X_MIX2)
            squares_f32(T_FFN2, 1)
            add_squares(xT, "x_ready", X_FFN2 + 8)


_INS = ("x", "norm_mix_pre", "norm_mix_post", "norm_ffn_pre", "norm_ffn_post", "w_in_first", "mu_shift", "attn_out_gain",
        "decay_w0", "decay_up", "aaa_a0", "aaa_up", "gate_up", "k_k", "k_a", "r_k", "gn_w", "gn_b", "w_out", "w_ffn_up",
        "w_ffn_down", "norm_mix_2", "w_in_2", "w_pool_2", "pool_scale_2", "w_out_2", "norm_mlp_2", "w_up_2", "w_down_2",
        "norm_final_2")


def kernel(**inputs):
    import concourse.bacc as bacc
    from concourse.bass_utils import run_bass_kernel_spmd

    nc = bacc.Bacc("TRN2", target_bir_lowering=False, num_devices=1)
    arrays, handles = {}, {}
    for name in _INS:
        array = np.ascontiguousarray(inputs[name])
        arrays[name + "_dram"] = array
        handles[name] = nc.dram_tensor(name + "_dram", array.shape, mybir.dt.from_np(array.dtype), kind="ExternalInput").ap()
    out = nc.dram_tensor("out_dram", (1, S, D), F32, kind="ExternalOutput").ap()
    program(nc, handles, out)
    return run_bass_kernel_spmd(nc, [arrays], core_ids=[0]).results[0]["out_dram"]
```
